# Optimizing a Trainium2 kernel written in Bass

```python
import jax, jax.numpy as jnp
from jax import lax
import numpy as np

D_MODEL = 1024
BATCH = 1
SEQ = 2048
DEPTH = 1

HEAD_DIM = 64
CONV_HEADS = 6
CONV_DIM = CONV_HEADS * HEAD_DIM
FOURIER_HEADS = 4
FOURIER_DIM = FOURIER_HEADS * HEAD_DIM
POOL_WINDOWS = (2, 4, 8, 16)
POOL_GROUPS = len(POOL_WINDOWS)
POOL_GROUP_DIM = 96
POOL_DIM = POOL_GROUPS * POOL_GROUP_DIM
MIX_DIM = CONV_DIM + FOURIER_DIM + POOL_DIM
IN_PROJ_DIM = 3 * CONV_DIM + FOURIER_DIM + POOL_DIM
CONV_WIDTH = 3
D_FF = ((8 * D_MODEL // 3 + 255) // 256) * 256
EPS = 1e-6

kernel_name = "hybrid_conv_fourier_pool_encoder"

def rmsnorm(x, g):
    xf = x.astype(jnp.float32)
    y = xf * lax.rsqrt(jnp.mean(xf * xf, axis=-1, keepdims=True) + EPS)
    return (y * g.astype(jnp.float32)).astype(x.dtype)

def short_gated_conv(b_gate, c_gate, h, w_conv):
    u = c_gate * h
    up = jnp.pad(u, ((0, 0), (1, 1), (0, 0)))
    s = u.shape[1]
    conv = (w_conv[0] * up[:, 0:s] + w_conv[1] * up[:, 1:s + 1] + w_conv[2] * up[:, 2:s + 2])
    return b_gate * conv

def fourier_mix(u, w_f):
    b, s, _ = u.shape
    uh = u.astype(jnp.float32).reshape(b, s, FOURIER_HEADS, HEAD_DIM)
    f = jnp.real(jnp.fft.fft2(uh, axes=(1, 3), norm="ortho")).astype(u.dtype)
    y = jnp.einsum("bshd,hde->bshe", f, w_f)
    return y.reshape(b, s, FOURIER_DIM)

def multiscale_pool(u, w_p, scale):
    b, s, _ = u.shape
    ug = u.reshape(b, s, POOL_GROUPS, POOL_GROUP_DIM)
    uf = ug.astype(jnp.float32)
    cs = jnp.concatenate([jnp.zeros((b, 1, POOL_GROUPS, POOL_GROUP_DIM), jnp.float32),
                          jnp.cumsum(uf, axis=1)], axis=1)
    t = jnp.arange(s)
    outs = []
    for g, w in enumerate(POOL_WINDOWS):
        lo = jnp.clip(t - w // 2, 0, s)
        hi = jnp.clip(t + w // 2, 0, s)
        cnt = (hi - lo).astype(jnp.float32)[None, :, None]
        mean = (cs[:, hi, g] - cs[:, lo, g]) / cnt
        outs.append(mean - uf[:, :, g])
    pooled = jnp.stack(outs, axis=2).astype(u.dtype)
    y = jnp.einsum("bsgd,gde->bsge", pooled, w_p).reshape(b, s, POOL_DIM)
    return y * scale

def swiglu(x, w1, w3, w2):
    return (jax.nn.silu(x @ w1) * (x @ w3)) @ w2

def setup_inputs(seed: int = 0) -> dict:
    key = jax.random.key(seed)
    ks = jax.random.split(key, 16)
    f32 = jnp.float32
    nrm = lambda k, shape, fan: jax.random.normal(k, shape, f32) * (fan ** -0.5)
    return {
        "x": jax.random.normal(ks[0], (BATCH, SEQ, D_MODEL), f32),
        "g_mix": 1.0 + 0.02 * jax.random.normal(ks[1], (DEPTH, D_MODEL), f32),
        "w_in": nrm(ks[2], (DEPTH, D_MODEL, IN_PROJ_DIM), D_MODEL),
        "w_conv": nrm(ks[3], (DEPTH, CONV_WIDTH, CONV_DIM), CONV_WIDTH),
        "w_fourier": nrm(ks[4], (DEPTH, FOURIER_HEADS, HEAD_DIM, HEAD_DIM), HEAD_DIM),
        "w_pool": nrm(ks[5], (DEPTH, POOL_GROUPS, POOL_GROUP_DIM, POOL_GROUP_DIM), POOL_GROUP_DIM),
        "pool_scale": 1.0 + 0.02 * jax.random.normal(ks[6], (DEPTH, POOL_DIM), f32),
        "w_out": nrm(ks[7], (DEPTH, MIX_DIM, D_MODEL), MIX_DIM),
        "g_ffn": 1.0 + 0.02 * jax.random.normal(ks[8], (DEPTH, D_MODEL), f32),
        "w1": nrm(ks[9], (DEPTH, D_MODEL, D_FF), D_MODEL),
        "w3": nrm(ks[10], (DEPTH, D_MODEL, D_FF), D_MODEL),
        "w2": nrm(ks[11], (DEPTH, D_FF, D_MODEL), D_FF),
        "g_final": 1.0 + 0.02 * jax.random.normal(ks[12], (D_MODEL,), f32),
    }

def reference(x, g_mix, w_in, w_conv, w_fourier, w_pool, pool_scale, w_out,
              g_ffn, w1, w3, w2, g_final):
    c0 = CONV_DIM
    for l in range(DEPTH):
        xn = rmsnorm(x, g_mix[l])
        z = xn @ w_in[l]
        b_gate = z[..., 0:c0]
        c_gate = z[..., c0:2 * c0]
        h = z[..., 2 * c0:3 * c0]
        u_f = z[..., 3 * c0:3 * c0 + FOURIER_DIM]
        u_p = z[..., 3 * c0 + FOURIER_DIM:]
        y_a = short_gated_conv(b_gate, c_gate, h, w_conv[l])
        y_b = fourier_mix(u_f, w_fourier[l])
        y_c = multiscale_pool(u_p, w_pool[l], pool_scale[l])
        y = jnp.concatenate([y_a, y_b, y_c], axis=-1)
        x = x + y @ w_out[l]
        x = x + swiglu(rmsnorm(x, g_ffn[l]), w1[l], w3[l], w2[l])
    return rmsnorm(x, g_final)


_drawn_inputs = setup_inputs


def setup_inputs(seed=0):
    import zlib

    import numpy as np

    out = dict(_drawn_inputs(seed))
    spreads = {}
    factors = {'g_mix': 2.682, 'pool_scale': 19.852, 'g_ffn': 20.891, 'g_final': 24.031}
    for name, (base, spread) in spreads.items():
        noise = np.random.default_rng([zlib.crc32(name.encode()), seed]).standard_normal(out[name].shape)
        drawn = base * np.exp(spread * noise) if base else spread * noise
        out[name] = __import__('jax').numpy.asarray(drawn.astype(out[name].dtype))
    for name, factor in factors.items():
        out[name] = (out[name] * factor).astype(out[name].dtype)
    return out
```

```python
import concourse.bass as bass
from concourse import mybir
from contextlib import ExitStack

P = 128
S = 2048
D = 1024
KT = D // P
NB = S // 512
CT = 3
FT = 2
CONV = CT * P
FOUR = FT * P
DFF = 2816
GF = 2
GROUPS = DFF // (P * GF)
TILES = S // P
R1 = 16
EPS = 1e-6
PAD = 8

F32 = mybir.dt.float32
F32R = mybir.dt.float32r
ALU = mybir.AluOpType
ACT = mybir.ActivationFunctionType


class Alloc:

    def __init__(self, nc):
        self.nc, self.stack = nc, ExitStack()

    def __enter__(self):
        self.stack.__enter__()
        return self

    def __exit__(self, *e):
        return self.stack.__exit__(*e)

    def sb(self, name, shape, dt=F32):
        return self.stack.enter_context(self.nc.sbuf_tensor(name, shape, dt))

    def pair(self, name, shape):
        return self.sb(name + "_hi", shape, F32R), self.sb(name + "_lo", shape, F32R)

    def sem(self, name):
        return self.stack.enter_context(self.nc.semaphore(name))

    def block(self):
        return self.stack.enter_context(self.nc.Block())


def mm3(nc, out, terms):
    last = len(terms) - 1
    for n, ((a_hi, a_lo), (b_hi, b_lo)) in enumerate(terms):
        nc.tensor.matmul(out, a_hi, b_hi, start=(n == 0), stop=False)
        nc.tensor.matmul(out, a_hi, b_lo, start=False, stop=False)
        ins = nc.tensor.matmul(out, a_lo, b_hi, start=False, stop=(n == last))
    return ins


def split_lo(nc, out, whole, hi):
    return nc.vector.tensor_tensor(out, whole, hi.bitcast(F32), ALU.subtract)


def stage_a(nc, t, ident, ps, uf):
    x_v = t["x"].rearrange("o (n p) d -> (o n) p d", p=P)
    w_v = t["w_in"].rearrange("o (k p) c -> p (o k) c", p=P)

    with Alloc(nc) as m:
        xT_hi, xT_lo = m.pair("xT", [P, KT, S])
        w_raw = m.sb("w_raw", [P, 3, KT, P])
        w_hi, w_lo = m.pair("w", [P, 3, KT, P])
        wconv = m.sb("wconv", [P, CT, 3])
        invw = m.sb("invw", [P, CT])
        invcnt = m.sb("invcnt", [P, CT, 2 * PAD])
        edge = m.sb("edge", [P, 2 * PAD])
        ss = m.sb("ss", [P, 2])
        rstd = m.sb("rstd", [P, 2])
        consts = m.sb("consts", [P, 2])
        bufs = m.sb("bufs", [P, 3, S + 2 * PAD])
        flat = bufs[:, :, :].rearrange("p a b -> p (a b)")
        x_in = flat[:, 0:2 * D].rearrange("p (s d) -> p s d", s=2)
        xn = flat[:, 2 * D:4 * D].rearrange("p (s d) -> p s d", s=2)
        g_b = flat[:, 4 * D:5 * D]
        X, U, Y = bufs[:, 0, :], bufs[:, 1, :], bufs[:, 2, :]
        core = slice(PAD, PAD + S)

        const_ld = m.sem("a_const_ld")
        x_ld = [m.sem(f"a_x_ld{i}") for i in range(2)]
        sq_done = m.sem("a_sq_done")
        consts_set = m.sem("a_consts_set")
        ms_done = m.sem("a_ms_done")
        rstd_done = m.sem("a_rstd_done")
        xn_done = m.sem("a_xn_done")
        tr_done = m.sem("a_tr_done")
        xhi_done = m.sem("a_xhi_done")
        xlo_done = m.sem("a_xlo_done")
        w_ld = [m.sem(f"a_w_ld{i}") for i in range(3)]
        whi_done = m.sem("a_whi_done")
        wlo_done = m.sem("a_wlo_done")
        z_mm = m.sem("a_z_mm")
        act_ev = m.sem("a_act_ev")
        dve_ev = m.sem("a_dve_ev")
        pad_set = m.sem("a_pad_set")
        tap0 = m.sem("a_tap0")
        tap1 = m.sem("a_tap1")
        tap2 = m.sem("a_tap2")
        conv_done = m.sem("a_conv_done")
        pstep = m.sem("a_pstep")
        pool_done = m.sem("a_pool_done")
        st_x = m.sem("a_st_x")
        st_u = m.sem("a_st_u")

        def col0(k):
            if isinstance(k, int) and k < 2:
                return 3 * CONV + k * P
            return 3 * CONV + FOUR + (k - 2) * P

        def load_w(sp, k, slot, col):
            sp.dma_start(w_raw[:, slot, :, :], w_v[:, :, bass.ds(col, P)]).then_inc(w_ld[slot], 16)

        block = m.block()

        @block.sync
        def _(sp):
            def x_load(n, s, first=False):
                if not first:
                    sp.wait_ge(xn_done, n - 1)
                sp.dma_start(x_in[:, s, :], x_v[bass.ds(n, 1), :, :].rearrange("o p d -> p (o d)")
                             ).then_inc(x_ld[s], 16)

            x_load(0, 0, True)
            sp.dma_start(g_b, t["g_mix"].to_broadcast([P, D])).then_inc(const_ld, 16)
            x_load(1, 1, True)
            sp.dma_start(ident[:, :], t["ident"]).then_inc(const_ld, 16)
            for k in range(3):
                load_w(sp, k, k, col0(k))
            sp.dma_start(wconv[:, :, :], t["wconv"]).then_inc(const_ld, 16)
            sp.dma_start(invw[:, :], t["invw"]).then_inc(const_ld, 16)
            sp.dma_start(invcnt[:, :, :], t["invcnt"]).then_inc(const_ld, 16)
            with sp.Fori(1, TILES // 2) as i:
                for s in range(2):
                    x_load(2 * i + s, s)
            for k in range(3, 5):
                sp.wait_ge(wlo_done, k - 2)
                load_w(sp, k, k % 3, col0(k))
            for q in range(CT):
                for r, base in enumerate((CONV, 2 * CONV, 0)):
                    k = 5 + 3 * q + r
                    sp.wait_ge(wlo_done, k - 2)
                    load_w(sp, k, k % 3, base + q * P)
                if q == 0:
                    for i in range(CT):
                        sp.wait_ge(pool_done, i + 1)
                        sp.dma_start(t["pooled"][:, i, :], U[:, core]).then_inc(st_u, 16)
                if q >= 1:
                    sp.wait_ge(conv_done, q)
                    sp.dma_start(t["yconv"][:, q - 1, :], X[:, core]).then_inc(st_x, 16)
            sp.wait_ge(conv_done, CT)
            sp.dma_start(t["yconv"][:, CT - 1, :], X[:, core]).then_inc(st_x, 16)
            sp.wait_ge(st_u, 16 * CT)
            sp.wait_ge(st_x, 16 * CT)

        @block.gpsimd
        def _(pool):
            nc.gpsimd.memset(consts[:, 0:1], -0.5)
            nc.gpsimd.memset(consts[:, 1:2], EPS).then_inc(consts_set, 1)
            pool.wait_ge(consts_set, 1)

            def rms(n, s):
                pool.wait_ge(sq_done, n + 1)
                nc.gpsimd.tensor_tensor(ss[:, s:s + 1], ss[:, s:s + 1], consts[:, 1:2], ALU.add).then_inc(ms_done, 1)
                pool.wait_ge(ms_done, n + 1)
                if not isinstance(n, int) or n >= 2:
                    pool.wait_ge(xn_done, n - 1)
                nc.gpsimd.tensor_tensor(rstd[:, s:s + 1], ss[:, s:s + 1], consts[:, 0:1], ALU.pow
                                        ).then_inc(rstd_done, 1)

            rms(0, 0)
            rms(1, 1)
            with pool.Fori(1, TILES // 2) as i:
                for s in range(2):
                    rms(2 * i + s, s)

        @block.scalar
        def _(act):
            def square(n, s):
                act.wait_ge(x_ld[s], 16)
                nc.scalar.activation(xn[:, s, :], x_in[:, s, :], ACT.Square, scale=D ** -0.5,
                                     accum_out=ss[:, s:s + 1]).then_inc(sq_done, 1)

            def x_hi(n, s):
                act.wait_ge(tr_done, n + 1)
                for b in range(2):
                    ins = nc.scalar.activation(xT_hi[:, 4 * b:4 * b + 4, bass.ds(n * P, P)],
                                               ps[:, 2 * s + b, :].rearrange("p (k t) -> p k t", k=4),
                                               ACT.Copy)
                ins.then_inc(xhi_done, 1)

            def square_i(i, s):
                act.wait_ge(x_ld[s], 16 * i + 16)
                act.wait_ge(tr_done, 2 * i + s - 1)
                act.wait_ge(rstd_done, 2 * i + s - 1)
                nc.scalar.activation(xn[:, s, :], x_in[:, s, :], ACT.Square, scale=D ** -0.5,
                                     accum_out=ss[:, s:s + 1]).then_inc(sq_done, 1)

            square(0, 0)
            square(1, 1)
            with act.Fori(0, TILES // 2 - 1) as i:
                for s in range(2):
                    x_hi(2 * i + s, s)
                    square_i(i + 1, s)
            for s in range(2):
                x_hi(TILES - 2 + s, s)

            def split_w(k):
                act.wait_ge(w_ld[k % 3], 16 * (k // 3 + 1))
                if k >= 3:
                    act.wait_ge(z_mm, NB * (k - 2))
                nc.scalar.activation(w_hi[:, k % 3, :, :], w_raw[:, k % 3, :, :], ACT.Copy
                                     ).then_inc(whi_done, 1)

            def evac(k, dst):
                for b in range(NB):
                    act.wait_ge(z_mm, NB * k + b + 1)
                    nc.scalar.activation(dst(b), ps[:, 4 + b, :], ACT.Copy).then_inc(act_ev, 1)

            act.wait_ge(const_ld, 80)
            split_w(0)
            for k in range(14):
                if k + 1 < 14:
                    split_w(k + 1)
                if k < 2:
                    evac(k, lambda b: uf[:, k, b * 512:(b + 1) * 512])
                elif k < 5:
                    if k == 2:
                        act.wait_ge(pad_set, 1)
                    else:
                        act.wait_ge(st_u, 16 * (k - 2))
                    evac(k, lambda b: U[:, PAD + b * 512:PAD + (b + 1) * 512])
                else:
                    q, r = divmod(k - 5, 3)
                    if r == 0:
                        if q == 0:
                            act.wait_ge(pool_done, CT)
                        else:
                            act.wait_ge(st_x, 16 * q)
                        evac(k, lambda b: X[:, PAD + b * 512:PAD + (b + 1) * 512])
                    elif r == 1:
                        act.wait_ge(dve_ev, NB * (q + 1))
                        nc.scalar.activation(X[:, core], U[:, PAD - 1:PAD - 1 + S], ACT.Copy,
                                             scale=wconv[:, q, 0:1]).then_inc(tap0, 1)
                    else:
                        if q >= 1:
                            act.wait_ge(conv_done, q)
                        evac(k, lambda b: Y[:, PAD + b * 512:PAD + (b + 1) * 512])

        @block.vector
        def _(dve):
            def norm(n, s):
                dve.wait_ge(rstd_done, n + 1)
                nc.vector.scalar_tensor_tensor(out=xn[:, s, :], in0=x_in[:, s, :],
                                               scalar=rstd[:, s:s + 1], in1=g_b, op0=ALU.mult,
                                               op1=ALU.mult).then_inc(xn_done, 1)

            def x_lo(n, s):
                dve.wait_ge(xhi_done, n + 1)
                for b in range(2):
                    sel = (slice(None), slice(4 * b, 4 * b + 4), bass.ds(n * P, P))
                    ins = split_lo(nc, xT_lo[sel], ps[:, 2 * s + b, :].rearrange("p (k t) -> p k t", k=4),
                                   xT_hi[sel])
                ins.then_inc(xlo_done, 1)

            dve.wait_ge(const_ld, 80)
            norm(0, 0)
            norm(1, 1)
            with dve.Fori(0, TILES // 2 - 1) as i:
                for s in range(2):
                    x_lo(2 * i + s, s)
                    norm(2 * i + 2 + s, s)
            for s in range(2):
                x_lo(TILES - 2 + s, s)

            dve.wait_ge(xn_done, TILES)
            dve.wait_ge(tr_done, TILES)
            nc.vector.memset(U[:, 0:PAD], 0.0)
            nc.vector.memset(U[:, PAD + S:], 0.0).then_inc(pad_set, 1)

            def split_w(k):
                dve.wait_ge(whi_done, k + 1)
                split_lo(nc, w_lo[:, k % 3, :, :], w_raw[:, k % 3, :, :], w_hi[:, k % 3, :, :]
                         ).then_inc(wlo_done, 1)

            steps = [0]

            def step(ins):
                steps[0] += 1
                ins.then_inc(pstep, 1)
                dve.wait_ge(pstep, steps[0])

            def double(dst, src, by, margin, parts):
                lo, hi = margin, S + 2 * PAD - margin
                for p0, p1 in parts:
                    step(nc.vector.tensor_tensor(dst[p0:p1, lo:hi], src[p0:p1, lo - by:hi - by],
                                                 src[p0:p1, lo + by:hi + by], ALU.add))

            def pooling(i):
                whole = [(0, P)]
                step(nc.vector.tensor_tensor(X[:, 1:], U[:, 0:S + 2 * PAD - 1], U[:, 1:], ALU.add))
                if i == 0:
                    double(Y, X, 1, 2, [(96, P)])
                    parts = [(0, 96, X), (96, P, Y)]
                elif i == 1:
                    double(Y, X, 1, 2, whole)
                    double(X, Y, 2, 4, [(64, P)])
                    parts = [(0, 64, Y), (64, P, X)]
                else:
                    double(Y, X, 1, 2, whole)
                    double(X, Y, 2, 4, whole)
                    double(Y, X, 4, 8, [(32, 64), (64, P)])
                    parts = [(0, 32, X), (32, 64, Y), (64, P, Y)]
                for p0, p1, w in parts:
                    inner = slice(2 * PAD, S)
                    step(nc.vector.scalar_tensor_tensor(
                        out=U[p0:p1, inner], in0=w[p0:p1, inner], scalar=invw[p0:p1, i:i + 1],
                        in1=U[p0:p1, inner], op0=ALU.mult, op1=ALU.subtract))
                    for e, c0 in enumerate((PAD, S)):
                        ed = edge[p0:p1, e * PAD:(e + 1) * PAD]
                        step(nc.vector.tensor_tensor(ed, w[p0:p1, c0:c0 + PAD],
                                                     invcnt[p0:p1, i, e * PAD:(e + 1) * PAD], ALU.mult))
                        step(nc.vector.tensor_tensor(U[p0:p1, c0:c0 + PAD], ed, U[p0:p1, c0:c0 + PAD],
                                                     ALU.subtract))
                nc.vector.tensor_copy(edge[:, 0:1], edge[:, 1:2]).then_inc(pool_done, 1)

            split_w(0)
            for k in range(14):
                if k + 1 < 14:
                    split_w(k + 1)
                if 2 <= k < 5:
                    dve.wait_ge(act_ev, NB * (k + 1))
                    pooling(k - 2)
                elif k >= 5:
                    q, r = divmod(k - 5, 3)
                    if r == 1:
                        if q == 0:
                            dve.wait_ge(st_u, 16 * CT)
                        dve.wait_ge(act_ev, NB * (6 + 2 * q))
                        for b in range(NB):
                            blk = slice(PAD + b * 512, PAD + (b + 1) * 512)
                            dve.wait_ge(z_mm, NB * k + b + 1)
                            nc.vector.tensor_tensor(U[:, blk], ps[:, 4 + b, :], X[:, blk], ALU.mult
                                                    ).then_inc(dve_ev, 1)
                    elif r == 2:
                        dve.wait_ge(tap0, q + 1)
                        dve.wait_ge(dve_ev, NB * (q + 1))
                        nc.vector.scalar_tensor_tensor(out=X[:, core], in0=U[:, core],
                                                       scalar=wconv[:, q, 1:2], in1=X[:, core],
                                                       op0=ALU.mult, op1=ALU.add).then_inc(tap1, 1)
                        dve.wait_ge(tap1, q + 1)
                        nc.vector.scalar_tensor_tensor(out=X[:, core], in0=U[:, PAD + 1:PAD + 1 + S],
                                                       scalar=wconv[:, q, 2:3], in1=X[:, core],
                                                       op0=ALU.mult, op1=ALU.add).then_inc(tap2, 1)
                        dve.wait_ge(tap2, q + 1)
                        dve.wait_ge(act_ev, NB * (7 + 2 * q))
                        nc.vector.tensor_tensor(X[:, core], X[:, core], Y[:, core], ALU.mult
                                                ).then_inc(conv_done, 1)

        @block.tensor
        def _(pe):
            def transposes(n, s):
                pe.wait_ge(xn_done, n + 1)
                if not isinstance(n, int) or n >= 2:
                    pe.wait_ge(xlo_done, n - 1)
                for k in range(KT):
                    ins = nc.tensor.transpose(ps[:, 2 * s + k // 4, (k % 4) * P:(k % 4 + 1) * P],
                                              xn[:, s, k * P:(k + 1) * P], ident[:, :])
                ins.then_inc(tr_done, 1)

            pe.wait_ge(const_ld, 80)
            transposes(0, 0)
            transposes(1, 1)
            with pe.Fori(1, TILES // 2) as i:
                for s in range(2):
                    transposes(2 * i + s, s)
            pe.wait_ge(xlo_done, TILES)

            for k in range(14):
                pe.wait_ge(wlo_done, k + 1)
                for b in range(NB):
                    if k >= 1:
                        q, r = divmod(k - 6, 3)
                        if k >= 7 and r == 1:
                            pe.wait_ge(dve_ev, NB * q + b + 1)
                        else:
                            n_act = k if k < 7 else k - (q if r < 1 else q + 1)
                            pe.wait_ge(act_ev, NB * (n_act - 1) + b + 1)
                    blk = slice(b * 512, (b + 1) * 512)
                    mm3(nc, ps[:, 4 + b, :],
                        [((w_hi[:, k % 3, c, :], w_lo[:, k % 3, c, :]),
                          (xT_hi[:, c, blk], xT_lo[:, c, blk])) for c in range(KT)]).then_inc(z_mm, 1)


def stage_b(nc, t, ps, uf, y):
    MB = P // 4
    tw_v = t["tw"]
    uf_v = uf[:, :, :].rearrange("p c (n r) -> p r c n", r=R1)
    CH = 8

    with Alloc(nc) as m:
        dft = m.sb("dft", [P, 2, P])
        wf = m.sb("wf", [P, FT, P])
        m_hi, m_lo = m.pair("m", [P, FT, 3 * P])
        us_hi, us_lo = m.pair("us", [P, 2, FT, P])
        tw = m.sb("tw_raw", [P, 2, 2, P])
        tw_hi, tw_lo = m.pair("tw", [P, 2, 2, P])
        ab_hi, ab_lo = m.pair("ab", [P, 2, FT, 3 * P])
        g = m.sb("g", [P, 2, FT * 2 * P])
        g3 = m.sb("g3", [P, FT, MB, P])
        g3_hi, g3_lo = m.pair("g3", [P, 2, CH * P])
        t16 = m.sb("t16_raw", [P, 64])
        t16_hi, t16_lo = m.pair("t16", [P, 64])
        wp = m.sb("wp_raw", [P, CT, CT * P])
        wp_hi, wp_lo = m.pair("wp", [P, CT, CT * P])
        pr = m.sb("pr", [P, 2, CT, 512])
        pr_hi, pr_lo = m.pair("pr", [P, CT, 512])
        pscale = m.sb("pscale", [P, CT])

        zeroed = m.sem("b_zeroed")
        c_ld = m.sem("b_c_ld")
        y_ld = m.sem("b_y_ld")
        tw_ld = [m.sem(f"b_tw_ld{i}") for i in range(2)]
        mix_mm = m.sem("b_mix_mm")
        mhi = m.sem("b_mhi")
        mlo = m.sem("b_mlo")
        prep_hi = m.sem("b_prep_hi")
        prep_lo = m.sem("b_prep_lo")
        f1_mm = m.sem("b_f1_mm")
        ab_h = m.sem("b_ab_h")
        ab_l = m.sem("b_ab_l")
        f2_mm = m.sem("b_f2_mm")
        g_ev = m.sem("b_g_ev")
        g_st = [m.sem(f"b_g_st{i}") for i in range(2)]
        pr_ld = [m.sem(f"b_pr_ld{i}") for i in range(2)]
        w2hi = m.sem("b_w2hi")
        w2lo = m.sem("b_w2lo")
        prh = m.sem("b_prh")
        prl = m.sem("b_prl")
        p_mm = m.sem("b_p_mm")
        p_ev = m.sem("b_p_ev")
        g3_ld = [m.sem(f"b_g3_ld{i}") for i in range(2)]
        g3h = m.sem("b_g3h")
        g3l = m.sem("b_g3l")
        f3_mm = m.sem("b_f3_mm")
        f3_ev = m.sem("b_f3_ev")

        block = m.block()
        pieces = [(j, r // P, r % P, r - 96 * j, n) for j in range(4)
                  for r, n in ([(0, 96)], [(96, 32), (128, 64)], [(192, 64), (256, 32)], [(288, 96)])[j]]
        NC = 3 + FT * 2 + len(pieces)

        @block.sync
        def _(sp):
            sp.dma_start(dft[:, :, :], t["dft64"]).then_inc(c_ld, 16)
            sp.wait_ge(zeroed, 2)
            for h in range(2 * FT):
                sp.dma_start(wf[64 * (h % 2):64 * (h % 2) + 64, h // 2, 64 * (h % 2):64 * (h % 2) + 64],
                             t["w_fourier"][0, h, :, :]).then_inc(c_ld, 16)
            for n in range(2):
                sp.dma_start(tw[:, n, :, :], tw_v[:, n, :, :]).then_inc(tw_ld[n], 16)
            sp.dma_start(t16[:, :], t["t16"]).then_inc(c_ld, 16)
            sp.dma_start(pscale[:, :], t["pscale"]).then_inc(c_ld, 16)
            for j, tile, p0, r0, n in pieces:
                sp.dma_start(wp[p0:p0 + n, tile, 96 * j:96 * j + 96], t["w_pool"][0, j, r0:r0 + n, :]
                             ).then_inc(c_ld, 16)
            for b in range(2):
                sp.dma_start(pr[:, b, :, :], t["pooled"][:, :, b * 512:(b + 1) * 512]).then_inc(pr_ld[b], 16)
            for e in range(2):
                sp.dma_start(y[:, 0:CT, e * D:(e + 1) * D], t["yconv"][:, :, e * D:(e + 1) * D]
                             ).then_inc(y_ld, 16)

            def g_store(n, s):
                sp.wait_ge(g_ev, n + 1)
                sp.dma_start(t["g"][:, :, bass.ds(n, 1), :].rearrange("c k o x -> k c (o x)"),
                             g[:, s, :].rearrange("p (c x) -> p c x", c=FT)).then_inc(g_st[s], 16)

            with sp.Fori(0, R1 // 2 - 1) as i:
                for s in range(2):
                    sp.wait_ge(prep_lo, 2 * i + s + 1)
                    sp.dma_start(tw[:, s, :, :], tw_v[:, bass.ds(2 * i + s + 2, 1), :, :].rearrange(
                        "p o a b -> p (o a) b")).then_inc(tw_ld[s], 16)
                for s in range(2):
                    g_store(2 * i + s, s)
            for s in range(2):
                g_store(R1 - 2 + s, s)
            for s in range(2):
                sp.wait_ge(g_st[s], 16 * R1 // 2)
            for c in range(FT):
                for a in range(4):
                    sp.dma_start(g3[32 * a:32 * a + 32, c, :, :],
                                 t["g"][c, 32 * a:32 * a + 32, :, :].rearrange(
                                     "b n (i x) -> (n i) b x", i=2)).then_inc(g3_ld[c], 16)
            for b in range(2, NB):
                sp.wait_ge(prl, b - 1)
                sp.dma_start(pr[:, b % 2, :, :], t["pooled"][:, :, b * 512:(b + 1) * 512]
                             ).then_inc(pr_ld[b % 2], 16)
            sp.wait_ge(y_ld, 32)

        @block.gpsimd
        def _(pool):
            nc.gpsimd.memset(wf[:, :, :], 0.0).then_inc(zeroed, 1)
            nc.gpsimd.memset(wp[:, :, :], 0.0).then_inc(zeroed, 1)

        @block.scalar
        def _(act):
            act.wait_ge(mix_mm, 1)
            for c in range(FT):
                nc.scalar.activation(m_hi[:, c, P:3 * P], ps[:, c, 0:2 * P], ACT.Copy)
                ins = nc.scalar.activation(m_hi[:, c, 0:P], ps[:, c, P:2 * P], ACT.Copy, scale=-1.0)
            ins.then_inc(mhi, 1)

            def prep(n, s, i=0):
                act.wait_ge(tw_ld[s], 16 * (i + 1))
                if not (isinstance(n, int) and n < 2):
                    act.wait_ge(f2_mm, n - 1)
                nc.scalar.activation(us_hi[:, s, :, :], uf_v[:, bass.ds(n, 1), :, :].rearrange(
                    "p o c n -> p (o c) n"), ACT.Copy)
                nc.scalar.activation(tw_hi[:, s, :, :], tw[:, s, :, :], ACT.Copy).then_inc(prep_hi, 1)

            def ab(n, s):
                act.wait_ge(f1_mm, n + 1)
                for c in range(FT):
                    ins = nc.scalar.activation(ab_hi[:, s, c, :], ps[:, 2 * s + c, 0:3 * P], ACT.Copy)
                ins.then_inc(ab_h, 1)

            prep(0, 0)
            prep(1, 1)
            with act.Fori(0, R1 // 2 - 1) as i:
                for s in range(2):
                    ab(2 * i + s, s)
                    prep(2 * i + 2 + s, s, i + 1)
            ab(R1 - 2, 0)
            ab(R1 - 1, 1)

            act.wait_ge(c_ld, 16 * NC)
            nc.scalar.activation(wp_hi[:, :, :], wp[:, :, :], ACT.Copy)
            nc.scalar.activation(t16_hi[:, :], t16[:, :], ACT.Copy).then_inc(w2hi, 1)

            def pr_split(b):
                act.wait_ge(pr_ld[b % 2], 16 * (b // 2 + 1))
                if b >= 1:
                    act.wait_ge(p_mm, CT * b)
                nc.scalar.activation(pr_hi[:, :, :], pr[:, b % 2, :, :], ACT.Copy).then_inc(prh, 1)

            for b in range(NB):
                pr_split(b)
                for o in range(CT):
                    act.wait_ge(p_mm, CT * b + o + 1)
                    nc.scalar.activation(y[:, CT + FT + o, b * 512:(b + 1) * 512], ps[:, 5 + o, :], ACT.Copy,
                                         scale=pscale[:, o:o + 1]).then_inc(p_ev, 1)

            def g3_split(j):
                if j % 4 == 0:
                    act.wait_ge(g3_ld[j // 4], 64)
                if j >= 2:
                    act.wait_ge(f3_mm, j - 1)
                nc.scalar.activation(g3_hi[:, j % 2, :], g3[:, j // 4, (j % 4) * CH:(j % 4 + 1) * CH, :
                                                            ].rearrange("p b x -> p (b x)"), ACT.Copy
                                     ).then_inc(g3h, 1)

            g3_split(0)
            g3_split(1)
            for j in range(4 * FT):
                act.wait_ge(f3_mm, j + 1)
                out = y[:, CT + j // 4, :].rearrange("p (m b) -> p b m", b=MB)[:, (j % 4) * CH:(j % 4 + 1) * CH, :]
                nc.scalar.activation(out, ps[:, j % 4, :].rearrange("p (b m) -> p b m", b=CH), ACT.Copy
                                     ).then_inc(f3_ev, 1)
                if j + 2 < 4 * FT:
                    g3_split(j + 2)

        @block.vector
        def _(dve):
            dve.wait_ge(mhi, 1)
            for c in range(FT):
                split_lo(nc, m_lo[:, c, P:3 * P], ps[:, c, 0:2 * P], m_hi[:, c, P:3 * P])
                ins = nc.vector.scalar_tensor_tensor(out=m_lo[:, c, 0:P], in0=ps[:, c, P:2 * P], scalar=-1.0,
                                                     in1=m_hi[:, c, 0:P].bitcast(F32), op0=ALU.mult,
                                                     op1=ALU.subtract)
            ins.then_inc(mlo, 1)

            def prep(n, s):
                dve.wait_ge(prep_hi, n + 1)
                split_lo(nc, us_lo[:, s, :, :], uf_v[:, bass.ds(n, 1), :, :].rearrange("p o c n -> p (o c) n"),
                         us_hi[:, s, :, :])
                split_lo(nc, tw_lo[:, s, :, :], tw[:, s, :, :], tw_hi[:, s, :, :]).then_inc(prep_lo, 1)

            def ab(n, s):
                dve.wait_ge(ab_h, n + 1)
                for c in range(FT):
                    ins = split_lo(nc, ab_lo[:, s, c, :], ps[:, 2 * s + c, 0:3 * P], ab_hi[:, s, c, :])
                ins.then_inc(ab_l, 1)

            def g_out(n, s, i=0):
                dve.wait_ge(f2_mm, n + 1)
                if not (isinstance(n, int) and n < 2):
                    dve.wait_ge(g_st[s], 16 * i)
                nc.vector.tensor_copy(g[:, s, :], ps[:, 4 + s, :]).then_inc(g_ev, 1)

            prep(0, 0)
            prep(1, 1)
            ab(0, 0)
            ab(1, 1)
            g_out(0, 0)
            g_out(1, 1)
            with dve.Fori(1, R1 // 2) as i:
                for s in range(2):
                    prep(2 * i + s, s)
                for s in range(2):
                    ab(2 * i + s, s)
                for s in range(2):
                    g_out(2 * i + s, s, i)

            dve.wait_ge(w2hi, 1)
            split_lo(nc, wp_lo[:, :, :], wp[:, :, :], wp_hi[:, :, :])
            split_lo(nc, t16_lo[:, :], t16[:, :], t16_hi[:, :]).then_inc(w2lo, 1)
            for b in range(NB):
                dve.wait_ge(prh, b + 1)
                split_lo(nc, pr_lo[:, :, :], pr[:, b % 2, :, :], pr_hi[:, :, :]).then_inc(prl, 1)
            for j in range(4 * FT):
                dve.wait_ge(g3h, j + 1)
                split_lo(nc, g3_lo[:, j % 2, :], g3[:, j // 4, (j % 4) * CH:(j % 4 + 1) * CH, :].rearrange(
                    "p b x -> p (b x)"), g3_hi[:, j % 2, :]).then_inc(g3l, 1)

        @block.tensor
        def _(pe):
            pe.wait_ge(c_ld, 16 * NC)
            for c in range(FT):
                for f in range(2):
                    ins = nc.tensor.matmul(ps[:, c, f * P:(f + 1) * P], dft[:, f, :], wf[:, c, :],
                                           start=True, stop=True)
            ins.then_inc(mix_mm, 1)
            pe.wait_ge(mlo, 1)

            def f1(n, s):
                pe.wait_ge(prep_lo, n + 1)
                if not (isinstance(n, int) and n < 2):
                    pe.wait_ge(ab_l, n - 1)
                for c in range(FT):
                    ins = mm3(nc, ps[:, 2 * s + c, 0:3 * P],
                              [((us_hi[:, s, c, :], us_lo[:, s, c, :]), (m_hi[:, c, :], m_lo[:, c, :]))])
                ins.then_inc(f1_mm, 1)

            def f2(n, s):
                pe.wait_ge(ab_l, n + 1)
                if not (isinstance(n, int) and n < 2):
                    pe.wait_ge(g_ev, n - 1)
                terms = [((tw_hi[:, s, f, :], tw_lo[:, s, f, :]),
                          (ab_hi[:, s, :, P - f * P:3 * P - f * P], ab_lo[:, s, :, P - f * P:3 * P - f * P]))
                         for f in range(2)]
                mm3(nc, ps[:, 4 + s, :].rearrange("p (c x) -> p c x", c=FT), terms).then_inc(f2_mm, 1)

            f1(0, 0)
            f1(1, 1)
            f2(0, 0)
            f2(1, 1)
            f1(2, 0)
            f1(3, 1)
            with pe.Fori(1, R1 // 2 - 1) as i:
                for s in range(2):
                    f2(2 * i + s, s)
                for s in range(2):
                    f1(2 * i + 2 + s, s)
            f2(R1 - 2, 0)
            f2(R1 - 1, 1)

            pe.wait_ge(w2lo, 1)
            for b in range(NB):
                pe.wait_ge(prl, b + 1)
                for o, tiles in enumerate(((0, 1), (0, 1, 2), (1, 2))):
                    if b >= 1:
                        pe.wait_ge(p_ev, CT * (b - 1) + o + 1)
                    elif o == 0:
                        pe.wait_ge(g_ev, R1)
                    mm3(nc, ps[:, 5 + o, :],
                        [((wp_hi[:, i, o * P:(o + 1) * P], wp_lo[:, i, o * P:(o + 1) * P]),
                          (pr_hi[:, i, :], pr_lo[:, i, :])) for i in tiles]).then_inc(p_mm, 1)

            for j in range(4 * FT):
                pe.wait_ge(g3l, j + 1)
                if j >= 4:
                    pe.wait_ge(f3_ev, j - 3)
                for b in range(CH):
                    ins = mm3(nc, ps[:, j % 4, b * 64:(b + 1) * 64],
                              [((g3_hi[:, j % 2, b * P:(b + 1) * P], g3_lo[:, j % 2, b * P:(b + 1) * P]),
                                (t16_hi[:, :], t16_lo[:, :]))])
                ins.then_inc(f3_mm, 1)


def stage_c(nc, t, ident, ps, y):
    x_v = t["x"].rearrange("o (n p) d -> (o n) p d", p=P)
    xm_v = t["xmid"]
    wo_v = t["w_out"].rearrange("o (k p) d -> (o k) p d", p=P)

    with Alloc(nc) as m:
        wo_raw = m.sb("wo_raw", [P, 2, D])
        wo_hi, wo_lo = m.pair("wo", [P, KT, D])
        ys_hi, ys_lo = m.pair("ys", [P, 2, KT, P])
        x_in = m.sb("cx_in", [P, 2, D])
        xm = m.sb("xm", [P, 2, D])
        xn = m.sb("cxn", [P, 2, D])
        xt = m.sb("xt", [P, 2, KT, P])
        g_b = m.sb("cg_b", [P, D])
        ss = m.sb("css", [P, 2])
        rstd = m.sb("crstd", [P, 2])
        consts = m.sb("cconsts", [P, 2])

        g_ld = m.sem("c_g_ld")
        wo_ld = [m.sem(f"c_wo_ld{i}") for i in range(2)]
        wo_h = m.sem("c_wo_h")
        wo_l = m.sem("c_wo_l")
        x_ld = [m.sem(f"c_x_ld{i}") for i in range(2)]
        ys_h = m.sem("c_ys_h")
        ys_l = m.sem("c_ys_l")
        o_mm = m.sem("c_o_mm")
        xm_done = m.sem("c_xm_done")
        consts_set = m.sem("c_consts_set")
        sq_done = m.sem("c_sq_done")
        ms_done = m.sem("c_ms_done")
        rstd_done = m.sem("c_rstd_done")
        xn_done = m.sem("c_xn_done")
        tr_done = m.sem("c_tr_done")
        xt_done = m.sem("c_xt_done")
        xm_st = [m.sem(f"c_xm_st{i}") for i in range(2)]
        xt_st = [m.sem(f"c_xt_st{i}") for i in range(2)]

        block = m.block()

        def later(n):
            return not (isinstance(n, int) and n < 2)

        @block.sync
        def _(sp):
            for k in range(KT):
                if k >= 2:
                    sp.wait_ge(wo_l, k - 1)
                sp.dma_start(wo_raw[:, k % 2, :], wo_v[k, :, :]).then_inc(wo_ld[k % 2], 16)
                if k == 1:
                    sp.dma_start(g_b[:, :], t["g_ffn"].to_broadcast([P, D])).then_inc(g_ld, 16)

            def x_load(n, s):
                if later(n):
                    sp.wait_ge(xm_done, 2 * n - 2)
                sp.dma_start(x_in[:, s, :], x_v[bass.ds(n, 1), :, :].rearrange("o p d -> p (o d)")
                             ).then_inc(x_ld[s], 16)

            def store(n, s):
                sp.wait_ge(xm_done, 2 * n + 2)
                sp.dma_start(xm_v[bass.ds(n, 1), :, :].rearrange("o p d -> p (o d)"), xm[:, s, :]
                             ).then_inc(xm_st[s], 16)
                sp.wait_ge(xt_done, n + 1)
                sp.dma_start(t["xt"][:, :, bass.ds(n * P, P)], xt[:, s, :, :]).then_inc(xt_st[s], 16)

            x_load(0, 0)
            x_load(1, 1)
            with sp.Fori(0, TILES // 2 - 1) as i:
                for s in range(2):
                    store(2 * i + s, s)
                    x_load(2 * i + 2 + s, s)
            for s in range(2):
                store(TILES - 2 + s, s)
            for s in range(2):
                sp.wait_ge(xm_st[s], 16 * TILES // 2)
                sp.wait_ge(xt_st[s], 16 * TILES // 2)

        @block.gpsimd
        def _(pool):
            nc.gpsimd.memset(consts[:, 0:1], -0.5)
            nc.gpsimd.memset(consts[:, 1:2], EPS).then_inc(consts_set, 1)
            pool.wait_ge(consts_set, 1)

            def rms(n, s):
                pool.wait_ge(sq_done, n + 1)
                nc.gpsimd.tensor_tensor(ss[:, s:s + 1], ss[:, s:s + 1], consts[:, 1:2], ALU.add).then_inc(ms_done, 1)
                pool.wait_ge(ms_done, n + 1)
                nc.gpsimd.tensor_tensor(rstd[:, s:s + 1], ss[:, s:s + 1], consts[:, 0:1], ALU.pow
                                        ).then_inc(rstd_done, 1)

            with pool.Fori(0, TILES // 2) as i:
                for s in range(2):
                    rms(2 * i + s, s)

        @block.scalar
        def _(act):
            for k in range(KT):
                act.wait_ge(wo_ld[k % 2], 16 * (k // 2 + 1))
                nc.scalar.activation(wo_hi[:, k, :], wo_raw[:, k % 2, :], ACT.Copy).then_inc(wo_h, 1)

            def ys(n, s):
                if later(n):
                    act.wait_ge(o_mm, 2 * n - 2)
                nc.scalar.activation(ys_hi[:, s, :, :], y[:, :, bass.ds(n * P, P)], ACT.Copy
                                     ).then_inc(ys_h, 1)

            def square(n, s):
                act.wait_ge(xm_done, 2 * n + 2)
                if later(n):
                    act.wait_ge(tr_done, n - 1)
                nc.scalar.activation(xn[:, s, :], xm[:, s, :], ACT.Square, scale=D ** -0.5, accum_out=ss[:, s:s + 1]
                                     ).then_inc(sq_done, 1)

            def evac(n, s, i=0):
                act.wait_ge(tr_done, n + 1)
                if later(n):
                    act.wait_ge(xt_st[s], 16 * i)
                for b in range(2):
                    ins = nc.scalar.activation(xt[:, s, 4 * b:4 * b + 4, :].rearrange("p k t -> p (k t)"),
                                               ps[:, 4 + 2 * s + b, :], ACT.Copy)
                ins.then_inc(xt_done, 1)

            ys(0, 0)
            ys(1, 1)
            for s in range(2):
                ys(2 + s, s)
                square(s, s)
                evac(s, s)
            with act.Fori(1, TILES // 2 - 1) as i:
                for s in range(2):
                    ys(2 * i + 2 + s, s)
                    square(2 * i + s, s)
                    evac(2 * i + s, s, i)
            for s in range(2):
                square(TILES - 2 + s, s)
                evac(TILES - 2 + s, s, TILES // 2 - 1)

        @block.vector
        def _(dve):
            for k in range(KT):
                dve.wait_ge(wo_h, k + 1)
                split_lo(nc, wo_lo[:, k, :], wo_raw[:, k % 2, :], wo_hi[:, k, :]).then_inc(wo_l, 1)
            dve.wait_ge(g_ld, 16)

            def ys(n, s):
                dve.wait_ge(ys_h, n + 1)
                split_lo(nc, ys_lo[:, s, :, :], y[:, :, bass.ds(n * P, P)], ys_hi[:, s, :, :]
                         ).then_inc(ys_l, 1)

            def residual(n, s, i=0):
                dve.wait_ge(x_ld[s], 16 * (i + 1))
                if later(n):
                    dve.wait_ge(xm_st[s], 16 * i)
                    dve.wait_ge(xn_done, n - 1)
                for b in range(2):
                    dve.wait_ge(o_mm, 2 * n + b + 1)
                    nc.vector.tensor_tensor(xm[:, s, b * 512:(b + 1) * 512], ps[:, 2 * s + b, :],
                                            x_in[:, s, b * 512:(b + 1) * 512], ALU.add
                                            ).then_inc(xm_done, 1)

            def norm(n, s):
                dve.wait_ge(rstd_done, n + 1)
                nc.vector.scalar_tensor_tensor(out=xn[:, s, :], in0=xm[:, s, :],
                                               scalar=rstd[:, s:s + 1], in1=g_b[:, :], op0=ALU.mult,
                                               op1=ALU.mult).then_inc(xn_done, 1)

            ys(0, 0)
            ys(1, 1)
            for s in range(2):
                residual(s, s)
                ys(2 + s, s)
                norm(s, s)
            with dve.Fori(1, TILES // 2 - 1) as i:
                for s in range(2):
                    residual(2 * i + s, s, i)
                    ys(2 * i + 2 + s, s)
                    norm(2 * i + s, s)
            for s in range(2):
                residual(TILES - 2 + s, s, TILES // 2 - 1)
                norm(TILES - 2 + s, s)

        @block.tensor
        def _(pe):
            pe.wait_ge(wo_l, KT)

            def products(n, s):
                pe.wait_ge(ys_l, n + 1)
                for b in range(2):
                    if later(n):
                        pe.wait_ge(xm_done, 2 * (n - 2) + b + 1)
                    mm3(nc, ps[:, 2 * s + b, :],
                        [((ys_hi[:, s, k, :], ys_lo[:, s, k, :]),
                          (wo_hi[:, k, b * 512:(b + 1) * 512], wo_lo[:, k, b * 512:(b + 1) * 512]))
                         for k in range(KT)]).then_inc(o_mm, 1)

            def transposes(n, s):
                pe.wait_ge(xn_done, n + 1)
                if later(n):
                    pe.wait_ge(xt_done, n - 1)
                for k in range(KT):
                    ins = nc.tensor.transpose(ps[:, 4 + 2 * s + k // 4, (k % 4) * P:(k % 4 + 1) * P],
                                              xn[:, s, k * P:(k + 1) * P], ident[:, :])
                ins.then_inc(tr_done, 1)

            products(0, 0)
            products(1, 1)
            transposes(0, 0)
            products(2, 0)
            transposes(1, 1)
            with pe.Fori(1, TILES // 2 - 1) as i:
                products(2 * i + 1, 1)
                transposes(2 * i, 0)
                products(2 * i + 2, 0)
                transposes(2 * i + 1, 1)
            products(TILES - 1, 1)
            transposes(TILES - 2, 0)
            transposes(TILES - 1, 1)


def stage_d(nc, t, ps, part):
    HT = TILES // 2
    T = HT * P
    w13_v = [t[w].rearrange("o (k p) f -> p (o k) f", p=P) for w in ("w1", "w3")]
    w2_v = t["w2"].rearrange("o (j p) d -> p (o j) d", p=P)
    FW = GF * P
    CHUNKS = 2 * KT // 2

    with Alloc(nc) as m:
        xf_hi, xf_lo = m.pair(f"xf{part}", [P, KT, T])
        xf_raw = m.sb(f"xf_raw{part}", [P, 2, 2, 512])
        w13_raw = m.sb(f"w13_raw{part}", [P, 2, KT, FW])
        w13_hi, w13_lo = m.pair(f"w13{part}", [P, GF, 2, KT, P])
        w2_raw = m.sb(f"w2_raw{part}", [P, GF, D])
        w2_hi, w2_lo = m.pair(f"w2{part}", [P, GF, D])
        h_hi, h_lo = m.pair(f"h{part}", [P, 2, GF, 512])
        sil = m.sb(f"sil{part}", [P, GF, 512])
        hf = m.sb(f"hf{part}", [P, GF, 512])
        acc = m.sb(f"acc{part}", [P, HT, D])
        ss = m.sb(f"dss{part}", [P, HT])
        rstd = m.sb(f"drstd{part}", [P, HT])
        consts = m.sb(f"dconsts{part}", [P, 2])
        g_b = sil[:, :, :].rearrange("p a b -> p (a b)")
        junk = hf[:, :, :].rearrange("p a b -> p (a b)")

        xf_ld = [m.sem(f"d_xf_ld{i}") for i in range(2)]
        xfh = m.sem("d_xfh")
        xfl = m.sem("d_xfl")
        w13_ld = [m.sem(f"d_w{i}_ld") for i in (1, 3)]
        w13h = m.sem("d_w13h")
        w13l = m.sem("d_w13l")
        w2_ld = m.sem("d_w2_ld")
        w2h = m.sem("d_w2h")
        w2l = m.sem("d_w2l")
        up_mm = m.sem("d_up_mm")
        sil_done = m.sem("d_sil_done")
        hf_done = m.sem("d_hf_done")
        hh = m.sem("d_hh")
        hl = m.sem("d_hl")
        dn_mm = m.sem("d_dn_mm")
        acc_done = m.sem("d_acc_done")
        g_ld = m.sem("d_g_ld")
        consts_set = m.sem("d_consts_set")
        sq_done = m.sem("d_sq_done")
        ms_done = m.sem("d_ms_done")
        rstd_done = m.sem("d_rstd_done")
        o_done = m.sem("d_o_done")
        o_st = m.sem("d_o_st")

        block = m.block()
        UB = GF
        DB = 8

        @block.sync
        def _(sp):
            def load13(i):
                for w in range(2):
                    sp.dma_start(w13_raw[:, w, :, :], w13_v[w][:, :, bass.ds(i * FW, FW)]
                                 ).then_inc(w13_ld[w], 16)

            def load2(i):
                sp.dma_start(w2_raw[:, :, :], w2_v[:, bass.ds(i * GF, GF), :]).then_inc(w2_ld, 16)

            load13(0)
            for c in range(CHUNKS):
                b, k = divmod(c, 4)
                if c >= 2:
                    sp.wait_ge(xfl, c - 1)
                sp.dma_start(xf_raw[:, c % 2, :, :],
                             t["xt"][:, 2 * k:2 * k + 2, part * T + b * 512:part * T + (b + 1) * 512]
                             ).then_inc(xf_ld[c % 2], 16)
            load2(0)
            sp.dma_start(acc[:, :, :], t["xmid"][part * HT:(part + 1) * HT, :, :].rearrange(
                "n p d -> p n d")).then_inc(acc_done, 16)
            with sp.Fori(1, GROUPS) as i:
                sp.wait_ge(w13l, GF * i)
                load13(i)
                sp.wait_ge(w2l, i)
                load2(i)
            sp.wait_ge(hf_done, 2 * UB * GROUPS)
            sp.dma_start(g_b, t["g_final"].to_broadcast([P, D])).then_inc(g_ld, 16)
            for n in range(HT):
                sp.wait_ge(o_done, n + 1)
                sp.dma_start(t["out"][0, (part * HT + n) * P:(part * HT + n + 1) * P, :], acc[:, n, :]
                             ).then_inc(o_st, 16)
            sp.wait_ge(o_st, 16 * HT)

        @block.gpsimd
        def _(pool):
            nc.gpsimd.memset(consts[:, 0:1], -0.5)
            nc.gpsimd.memset(consts[:, 1:2], EPS).then_inc(consts_set, 1)
            pool.wait_ge(consts_set, 1)
            for n in range(HT):
                pool.wait_ge(sq_done, n + 1)
                nc.gpsimd.tensor_tensor(ss[:, n:n + 1], ss[:, n:n + 1], consts[:, 1:2], ALU.add).then_inc(ms_done, 1)
                pool.wait_ge(ms_done, n + 1)
                nc.gpsimd.tensor_tensor(rstd[:, n:n + 1], ss[:, n:n + 1], consts[:, 0:1], ALU.pow
                                        ).then_inc(rstd_done, 1)

        @block.scalar
        def _(act):
            def w13_split(i, f):
                for w in range(2):
                    act.wait_ge(w13_ld[w], 16 * i + 16)
                if not isinstance(i, int) or i:
                    act.wait_ge(up_mm, 2 * UB * i - UB + f + 1)
                for w in range(2):
                    ins = nc.scalar.activation(w13_hi[:, f, w, :, :], w13_raw[:, w, :, f * P:(f + 1) * P],
                                               ACT.Copy)
                ins.then_inc(w13h, 1)

            def w2_split(i):
                act.wait_ge(w2_ld, 16 * i + 16)
                if not isinstance(i, int) or i:
                    act.wait_ge(dn_mm, 2 * DB * i)
                nc.scalar.activation(w2_hi[:, :, :], w2_raw[:, :, :], ACT.Copy).then_inc(w2h, 1)

            def activate(i, b, f):
                n = 2 * UB * i + UB * b + f
                act.wait_ge(up_mm, n + 1)
                if not isinstance(i, int) or n >= GF:
                    act.wait_ge(hf_done, n - 1)
                nc.scalar.activation(sil[:, f, :], ps[:, 2 * f, :], ACT.Silu).then_inc(sil_done, 1)
                act.wait_ge(hf_done, n + 1)
                nc.scalar.activation(h_hi[:, b, f, :], hf[:, f, :], ACT.Copy).then_inc(hh, 1)

            w13_split(0, 0)
            for c in range(CHUNKS):
                b, k = divmod(c, 4)
                act.wait_ge(xf_ld[c % 2], 16 * (c // 2 + 1))
                nc.scalar.activation(xf_hi[:, 2 * k:2 * k + 2, b * 512:(b + 1) * 512],
                                     xf_raw[:, c % 2, :, :], ACT.Copy).then_inc(xfh, 1)
                if c == 3:
                    w13_split(0, 1)
            w2_split(0)
            for f in range(GF):
                activate(0, 0, f)

            def group(i, more):
                for f in range(GF):
                    activate(i, 1, f)
                    if more:
                        w13_split(i + 1, f)
                if more:
                    for f in range(GF):
                        activate(i + 1, 0, f)
                    w2_split(i + 1)

            with act.Fori(0, GROUPS - 1) as i:
                group(i, True)
            group(GROUPS - 1, False)

            for n in range(HT):
                act.wait_ge(acc_done, 16 + 2 * DB * (GROUPS - 1) + 2 * n + 2)
                if n:
                    act.wait_ge(sq_done, n)
                nc.scalar.activation(junk, acc[:, n, :], ACT.Square, scale=D ** -0.5, accum_out=ss[:, n:n + 1]
                                     ).then_inc(sq_done, 1)

        @block.vector
        def _(dve):
            def w13_split(i, f):
                dve.wait_ge(w13h, GF * i + f + 1)
                for w in range(2):
                    ins = split_lo(nc, w13_lo[:, f, w, :, :], w13_raw[:, w, :, f * P:(f + 1) * P],
                                   w13_hi[:, f, w, :, :])
                ins.then_inc(w13l, 1)

            def w2_split(i):
                dve.wait_ge(w2h, i + 1)
                split_lo(nc, w2_lo[:, :, :], w2_raw[:, :, :], w2_hi[:, :, :]).then_inc(w2l, 1)

            def activate(i, b, f):
                n = 2 * UB * i + UB * b + f
                dve.wait_ge(sil_done, n + 1)
                if not isinstance(i, int) or n >= GF:
                    dve.wait_ge(hl, n - 1)
                nc.vector.tensor_tensor(hf[:, f, :], ps[:, 2 * f + 1, :], sil[:, f, :], ALU.mult
                                        ).then_inc(hf_done, 1)
                dve.wait_ge(hh, n + 1)
                split_lo(nc, h_lo[:, b, f, :], hf[:, f, :], h_hi[:, b, f, :]).then_inc(hl, 1)

            def add(i, b):
                for j in range(DB):
                    n = 2 * DB * i + DB * b + j
                    dve.wait_ge(dn_mm, n + 1)
                    dve.wait_ge(acc_done, max(16, n + 17 - 2 * DB) if isinstance(i, int) else n + 17 - 2 * DB)
                    part_of = acc[:, 4 * b + j // 2, (j % 2) * 512:(j % 2 + 1) * 512]
                    nc.vector.tensor_tensor(part_of, ps[:, 4 + j % 4, :], part_of, ALU.add
                                            ).then_inc(acc_done, 1)

            w13_split(0, 0)
            for c in range(CHUNKS):
                b, k = divmod(c, 4)
                dve.wait_ge(xfh, c + 1)
                sel = (slice(None), slice(2 * k, 2 * k + 2), slice(b * 512, (b + 1) * 512))
                split_lo(nc, xf_lo[sel], xf_raw[:, c % 2, :, :], xf_hi[sel]).then_inc(xfl, 1)
                if c == 3:
                    w13_split(0, 1)
            w2_split(0)
            dve.wait_ge(acc_done, 16)
            for f in range(GF):
                activate(0, 0, f)

            def group(i, more):
                for f in range(GF):
                    activate(i, 1, f)
                    if more:
                        w13_split(i + 1, f)
                add(i, 0)
                if more:
                    for f in range(GF):
                        activate(i + 1, 0, f)
                add(i, 1)
                if more:
                    w2_split(i + 1)

            with dve.Fori(0, GROUPS - 1) as i:
                group(i, True)
            group(GROUPS - 1, False)

            dve.wait_ge(g_ld, 16)
            for n in range(HT):
                dve.wait_ge(rstd_done, n + 1)
                nc.vector.scalar_tensor_tensor(out=acc[:, n, :], in0=acc[:, n, :], scalar=rstd[:, n:n + 1],
                                               in1=g_b, op0=ALU.mult, op1=ALU.mult).then_inc(o_done, 1)

        @block.tensor
        def _(pe):
            def up(i, b):
                for f in range(GF):
                    n = 2 * UB * i + UB * b + f
                    if b == 0:
                        pe.wait_ge(w13l, GF * i + f + 1)
                    for w in range(2):
                        if not isinstance(i, int) or n >= GF:
                            pe.wait_ge((sil_done, hf_done)[w], n - 1)
                        if isinstance(i, int) and i == 0 and f == 0 and w == 0:
                            pe.wait_ge(xfl, 4 * b + 4)
                        ins = mm3(nc, ps[:, 2 * f + w, :],
                                  [((w13_hi[:, f, w, k, :], w13_lo[:, f, w, k, :]),
                                    (xf_hi[:, k, b * 512:(b + 1) * 512], xf_lo[:, k, b * 512:(b + 1) * 512]))
                                   for k in range(KT)])
                    ins.then_inc(up_mm, 1)

            def down(i, b):
                pe.wait_ge(hl, 2 * UB * i + UB * b + UB)
                if b == 0:
                    pe.wait_ge(w2l, i + 1)
                for j in range(DB):
                    n = 2 * DB * i + DB * b + j
                    if not isinstance(i, int) or n >= 4:
                        pe.wait_ge(acc_done, n + 13)
                    tok = slice((j // 2) * P, (j // 2 + 1) * P)
                    col = slice((j % 2) * 512, (j % 2 + 1) * 512)
                    mm3(nc, ps[:, 4 + j % 4, :],
                        [((h_hi[:, b, f, tok], h_lo[:, b, f, tok]), (w2_hi[:, f, col], w2_lo[:, f, col]))
                         for f in range(GF)]).then_inc(dn_mm, 1)

            up(0, 0)
            up(0, 1)
            down(0, 0)
            up(1, 0)
            down(0, 1)
            with pe.Fori(1, GROUPS - 1) as i:
                up(i, 1)
                down(i, 0)
                up(i + 1, 0)
                down(i, 1)
            up(GROUPS - 1, 1)
            down(GROUPS - 1, 0)
            down(GROUPS - 1, 1)


def encoder_layer(nc, t):
    with Alloc(nc) as m:
        ident = m.sb("ident", [P, P])
        ps = m.stack.enter_context(nc.psum_tensor("ps", [P, 8, 512], F32))
        with Alloc(nc) as mu:
            uf = mu.sb("uf", [P, FT, S])
            stage_a(nc, t, ident, ps, uf)
            with Alloc(nc) as my:
                y = my.sb("y_b", [P, KT, S])
                stage_b(nc, t, ps, uf, y)
                stage_c(nc, t, ident, ps, y)
        for part in range(2):
            stage_d(nc, t, ps, part)


def shape_constants():
    import numpy as np
    hd = 64
    j = np.arange(hd)
    ang = 2 * np.pi * np.outer(j, j) / hd
    norm = 1.0 / np.sqrt(S * hd)
    dft64 = np.zeros((P, 2, P))
    for f, mat in enumerate((np.cos(ang), np.sin(ang))):
        for h in range(2):
            dft64[hd * h:hd * h + hd, f, hd * h:hd * h + hd] = mat * norm
    n2 = np.arange(P)[:, None, None]
    n1 = np.arange(R1)[None, :, None]
    k2 = np.arange(P)[None, None, :]
    ang = 2 * np.pi * (((n1 + R1 * n2) * k2) % S) / S
    tw = np.stack([np.cos(ang), np.sin(ang)], axis=2)
    t16 = np.zeros((4, R1, 2, R1, 4))
    k1 = np.arange(R1)
    ang = 2 * np.pi * (np.outer(k1, k1) % R1) / R1
    for a in range(4):
        t16[a, :, 0, :, a] = np.cos(ang)
        t16[a, :, 1, :, a] = -np.sin(ang)
    windows = np.repeat([2, 4, 8, 16], 96)
    tok = np.concatenate([np.arange(PAD), np.arange(S - PAD, S)])
    cnt = (np.minimum(tok + windows[:, None] // 2, S) - np.maximum(tok - windows[:, None] // 2, 0))
    f = np.float32
    return {
        "ident": np.eye(P, dtype=f), "dft64": dft64.astype(f), "tw": tw.astype(f),
        "t16": t16.reshape(P, 64).astype(f),
        "invw": np.ascontiguousarray((1.0 / windows).reshape(CT, P).T).astype(f),
        "invcnt": np.ascontiguousarray((1.0 / cnt).reshape(CT, P, 2 * PAD).transpose(1, 0, 2)).astype(f),
    }


_INS = ["x", "g_mix", "w_in", "w_fourier", "w_pool", "w_out", "g_ffn", "w1", "w3", "w2"]


def kernel(**inputs):
    import numpy as np
    import concourse.bacc as bacc
    from concourse.bass_utils import run_bass_kernel_spmd

    nc = bacc.Bacc("TRN2", target_bir_lowering=False, num_devices=1)
    arrays = {n: np.ascontiguousarray(inputs[n]) for n in _INS}
    arrays["g_final"] = np.ascontiguousarray(inputs["g_final"]).reshape(1, D)
    arrays["wconv"] = np.ascontiguousarray(np.asarray(inputs["w_conv"]).reshape(3, CT, P).transpose(2, 1, 0))
    arrays["pscale"] = np.ascontiguousarray(np.asarray(inputs["pool_scale"]).reshape(CT, P).T)
    arrays.update(shape_constants())
    t = {n: nc.dram_tensor(f"in_{n}", a.shape, mybir.dt.from_np(a.dtype), kind="ExternalInput").ap()
         for n, a in arrays.items()}
    t["out"] = nc.dram_tensor("out", (1, S, D), F32, kind="ExternalOutput").ap()
    for n, shape in (("yconv", (P, CT, S)), ("pooled", (P, CT, S)), ("g", (FT, P, R1, 2 * P)),
                     ("xmid", (TILES, P, D)), ("xt", (P, KT, S))):
        t[n] = nc.dram_tensor(f"scratch_{n}", shape, F32, kind="Internal").ap()
    encoder_layer(nc, t)
    r = run_bass_kernel_spmd(nc, [{f"in_{n}": a for n, a in arrays.items()}], core_ids=[0])
    return r.results[0]["out"]
```

```python
import concourse.bass as bass
from concourse import mybir
from contextlib import ExitStack

P = 128
S = 2048
HS = S // 2
D = 1024
KT = D // P
NB = S // 512
CT = 3
FT = 2
CONV = CT * P
FOUR = FT * P
DFF = 2816
GF = 2
GROUPS = DFF // (P * GF)
TILES = S // P
R1 = 16
EPS = 1e-6
PAD = 8

F32 = mybir.dt.float32
F32R = mybir.dt.float32r
ALU = mybir.AluOpType
ACT = mybir.ActivationFunctionType


class Alloc:

    def __init__(self, nc):
        self.nc, self.stack = nc, ExitStack()

    def __enter__(self):
        self.stack.__enter__()
        return self

    def __exit__(self, *e):
        return self.stack.__exit__(*e)

    def sb(self, name, shape, dt=F32, side=None):
        return self.stack.enter_context(self.nc.sbuf_tensor(name, shape, dt, side=side))

    def pair(self, name, shape):
        return self.sb(name + "_hi", shape, F32R), self.sb(name + "_lo", shape, F32R)

    def sem(self, name):
        return self.stack.enter_context(self.nc.semaphore(name))

    def block(self):
        return self.stack.enter_context(self.nc.Block())


def mm3(nc, out, terms):
    last = len(terms) - 1
    for n, ((a_hi, a_lo), (b_hi, b_lo)) in enumerate(terms):
        nc.tensor.matmul(out, a_hi, b_hi, start=(n == 0), stop=False)
        nc.tensor.matmul(out, a_hi, b_lo, start=False, stop=False)
        ins = nc.tensor.matmul(out, a_lo, b_hi, start=False, stop=(n == last))
    return ins


def split_lo(nc, out, whole, hi):
    return nc.vector.tensor_tensor(out, whole, hi.bitcast(F32), ALU.subtract)


def stage_a(nc, t, ident, ps, uf):
    x_v = t["x"].rearrange("o (n p) d -> (o n) p d", p=P)
    w_v = t["w_in"].rearrange("o (k p) c -> p (o k) c", p=P)

    with Alloc(nc) as m:
        xT_hi, xT_lo = m.pair("xT", [P, KT, S])
        w_raw = m.sb("w_raw", [P, 3, KT, P])
        w_hi, w_lo = m.pair("w", [P, 3, KT, P])
        wconv = m.sb("wconv", [P, CT, 3])
        invw = m.sb("invw", [P, CT])
        invcnt = m.sb("invcnt", [P, CT, 2 * PAD])
        edge = m.sb("edge", [P, 2 * PAD])
        ss = m.sb("ss", [P, 2])
        rstd = m.sb("rstd", [P, 2])
        consts = m.sb("consts", [P, 2])
        bufs = m.sb("bufs", [P, 3, S + 2 * PAD])
        flat = bufs[:, :, :].rearrange("p a b -> p (a b)")
        x_in = flat[:, 0:2 * D].rearrange("p (s d) -> p s d", s=2)
        xn = flat[:, 2 * D:4 * D].rearrange("p (s d) -> p s d", s=2)
        g_b = flat[:, 4 * D:5 * D]
        X, U, Y = bufs[:, 0, :], bufs[:, 1, :], bufs[:, 2, :]
        core = slice(PAD, PAD + S)

        const_ld = m.sem("a_const_ld")
        x_ld = [m.sem(f"a_x_ld{i}") for i in range(2)]
        sq_done = m.sem("a_sq_done")
        consts_set = m.sem("a_consts_set")
        ms_done = m.sem("a_ms_done")
        rstd_done = m.sem("a_rstd_done")
        xn_done = m.sem("a_xn_done")
        tr_done = m.sem("a_tr_done")
        xhi_done = m.sem("a_xhi_done")
        xlo_done = m.sem("a_xlo_done")
        w_ld = [m.sem(f"a_w_ld{i}") for i in range(3)]
        whi_done = m.sem("a_whi_done")
        wlo_done = m.sem("a_wlo_done")
        z_mm = m.sem("a_z_mm")
        act_ev = m.sem("a_act_ev")
        dve_ev = m.sem("a_dve_ev")
        pad_set = m.sem("a_pad_set")
        tap0 = m.sem("a_tap0")
        tap1 = m.sem("a_tap1")
        tap2 = m.sem("a_tap2")
        conv_done = m.sem("a_conv_done")
        pstep = m.sem("a_pstep")
        pool_done = m.sem("a_pool_done")
        st_x = m.sem("a_st_x")
        st_u = m.sem("a_st_u")

        def col0(k):
            if isinstance(k, int) and k < 2:
                return 3 * CONV + k * P
            return 3 * CONV + FOUR + (k - 2) * P

        def load_w(sp, k, slot, col):
            sp.dma_start(w_raw[:, slot, :, :], w_v[:, :, bass.ds(col, P)]).then_inc(w_ld[slot], 16)

        block = m.block()

        @block.sync
        def _(sp):
            def x_load(n, s, first=False):
                if not first:
                    sp.wait_ge(xn_done, n - 1)
                sp.dma_start(x_in[:, s, :], x_v[bass.ds(n, 1), :, :].rearrange("o p d -> p (o d)")
                             ).then_inc(x_ld[s], 16)

            x_load(0, 0, True)
            sp.dma_start(g_b, t["g_mix"].to_broadcast([P, D])).then_inc(const_ld, 16)
            x_load(1, 1, True)
            sp.dma_start(ident[:, :], t["ident"]).then_inc(const_ld, 16)
            for k in range(3):
                load_w(sp, k, k, col0(k))
            sp.dma_start(wconv[:, :, :], t["wconv"]).then_inc(const_ld, 16)
            sp.dma_start(invw[:, :], t["invw"]).then_inc(const_ld, 16)
            sp.dma_start(invcnt[:, :, :], t["invcnt"]).then_inc(const_ld, 16)
            with sp.Fori(1, TILES // 2) as i:
                for s in range(2):
                    x_load(2 * i + s, s)
            for k in range(3, 5):
                sp.wait_ge(wlo_done, k - 2)
                load_w(sp, k, k % 3, col0(k))
            for q in range(CT):
                for r, base in enumerate((CONV, 2 * CONV, 0)):
                    k = 5 + 3 * q + r
                    sp.wait_ge(wlo_done, k - 2)
                    load_w(sp, k, k % 3, base + q * P)
                if q == 0:
                    for i in range(CT):
                        sp.wait_ge(pool_done, i + 1)
                        sp.dma_start(t["pooled"][:, i, :], U[:, core]).then_inc(st_u, 16)
                if q >= 1:
                    sp.wait_ge(conv_done, q)
                    sp.dma_start(t["yconv"][:, q - 1, :], X[:, core]).then_inc(st_x, 16)
            sp.wait_ge(conv_done, CT)
            sp.dma_start(t["yconv"][:, CT - 1, :], X[:, core]).then_inc(st_x, 16)
            sp.wait_ge(st_u, 16 * CT)
            sp.wait_ge(st_x, 16 * CT)

        @block.gpsimd
        def _(pool):
            nc.gpsimd.memset(consts[:, 0:1], -0.5)
            nc.gpsimd.memset(consts[:, 1:2], EPS).then_inc(consts_set, 1)
            pool.wait_ge(consts_set, 1)

            def rms(n, s):
                pool.wait_ge(sq_done, n + 1)
                nc.gpsimd.tensor_tensor(ss[:, s:s + 1], ss[:, s:s + 1], consts[:, 1:2], ALU.add).then_inc(ms_done, 1)
                pool.wait_ge(ms_done, n + 1)
                if not isinstance(n, int) or n >= 2:
                    pool.wait_ge(xn_done, n - 1)
                nc.gpsimd.tensor_tensor(rstd[:, s:s + 1], ss[:, s:s + 1], consts[:, 0:1], ALU.pow
                                        ).then_inc(rstd_done, 1)

            rms(0, 0)
            rms(1, 1)
            with pool.Fori(1, TILES // 2) as i:
                for s in range(2):
                    rms(2 * i + s, s)

        @block.scalar
        def _(act):
            def square(n, s):
                act.wait_ge(x_ld[s], 16)
                nc.scalar.activation(xn[:, s, :], x_in[:, s, :], ACT.Square, scale=D ** -0.5,
                                     accum_out=ss[:, s:s + 1]).then_inc(sq_done, 1)

            def x_hi(n, s):
                act.wait_ge(tr_done, n + 1)
                for b in range(2):
                    ins = nc.scalar.activation(xT_hi[:, 4 * b:4 * b + 4, bass.ds(n * P, P)],
                                               ps[:, 2 * s + b, :].rearrange("p (k t) -> p k t", k=4),
                                               ACT.Copy)
                ins.then_inc(xhi_done, 1)

            def square_i(i, s):
                act.wait_ge(x_ld[s], 16 * i + 16)
                act.wait_ge(tr_done, 2 * i + s - 1)
                act.wait_ge(rstd_done, 2 * i + s - 1)
                nc.scalar.activation(xn[:, s, :], x_in[:, s, :], ACT.Square, scale=D ** -0.5,
                                     accum_out=ss[:, s:s + 1]).then_inc(sq_done, 1)

            square(0, 0)
            square(1, 1)
            with act.Fori(0, TILES // 2 - 1) as i:
                for s in range(2):
                    x_hi(2 * i + s, s)
                    square_i(i + 1, s)
            for s in range(2):
                x_hi(TILES - 2 + s, s)

            def split_w(k):
                act.wait_ge(w_ld[k % 3], 16 * (k // 3 + 1))
                if k >= 3:
                    act.wait_ge(z_mm, NB * (k - 2))
                nc.scalar.activation(w_hi[:, k % 3, :, :], w_raw[:, k % 3, :, :], ACT.Copy
                                     ).then_inc(whi_done, 1)

            def evac(k, dst):
                for b in range(NB):
                    act.wait_ge(z_mm, NB * k + b + 1)
                    nc.scalar.activation(dst(b), ps[:, 4 + b, :], ACT.Copy).then_inc(act_ev, 1)

            act.wait_ge(const_ld, 80)
            split_w(0)
            for k in range(14):
                if k + 1 < 14:
                    split_w(k + 1)
                if k < 2:
                    evac(k, lambda b: uf[:, k, b * 512:(b + 1) * 512])
                elif k < 5:
                    if k == 2:
                        act.wait_ge(pad_set, 1)
                    else:
                        act.wait_ge(st_u, 16 * (k - 2))
                    evac(k, lambda b: U[:, PAD + b * 512:PAD + (b + 1) * 512])
                else:
                    q, r = divmod(k - 5, 3)
                    if r == 0:
                        if q == 0:
                            act.wait_ge(pool_done, CT)
                        else:
                            act.wait_ge(st_x, 16 * q)
                        evac(k, lambda b: X[:, PAD + b * 512:PAD + (b + 1) * 512])
                    elif r == 1:
                        act.wait_ge(dve_ev, NB * (q + 1))
                        nc.scalar.activation(X[:, core], U[:, PAD - 1:PAD - 1 + S], ACT.Copy,
                                             scale=wconv[:, q, 0:1]).then_inc(tap0, 1)
                    else:
                        if q >= 1:
                            act.wait_ge(conv_done, q)
                        evac(k, lambda b: Y[:, PAD + b * 512:PAD + (b + 1) * 512])

        @block.vector
        def _(dve):
            def norm(n, s):
                dve.wait_ge(rstd_done, n + 1)
                nc.vector.scalar_tensor_tensor(out=xn[:, s, :], in0=x_in[:, s, :],
                                               scalar=rstd[:, s:s + 1], in1=g_b, op0=ALU.mult,
                                               op1=ALU.mult).then_inc(xn_done, 1)

            def x_lo(n, s):
                dve.wait_ge(xhi_done, n + 1)
                for b in range(2):
                    sel = (slice(None), slice(4 * b, 4 * b + 4), bass.ds(n * P, P))
                    ins = split_lo(nc, xT_lo[sel], ps[:, 2 * s + b, :].rearrange("p (k t) -> p k t", k=4),
                                   xT_hi[sel])
                ins.then_inc(xlo_done, 1)

            dve.wait_ge(const_ld, 80)
            norm(0, 0)
            norm(1, 1)
            with dve.Fori(0, TILES // 2 - 1) as i:
                for s in range(2):
                    x_lo(2 * i + s, s)
                    norm(2 * i + 2 + s, s)
            for s in range(2):
                x_lo(TILES - 2 + s, s)

            dve.wait_ge(xn_done, TILES)
            dve.wait_ge(tr_done, TILES)
            nc.vector.memset(U[:, 0:PAD], 0.0)
            nc.vector.memset(U[:, PAD + S:], 0.0).then_inc(pad_set, 1)

            def split_w(k):
                dve.wait_ge(whi_done, k + 1)
                split_lo(nc, w_lo[:, k % 3, :, :], w_raw[:, k % 3, :, :], w_hi[:, k % 3, :, :]
                         ).then_inc(wlo_done, 1)

            steps = [0]

            def step(ins):
                steps[0] += 1
                ins.then_inc(pstep, 1)
                dve.wait_ge(pstep, steps[0])

            def double(dst, src, by, margin, parts):
                lo, hi = margin, S + 2 * PAD - margin
                for p0, p1 in parts:
                    step(nc.vector.tensor_tensor(dst[p0:p1, lo:hi], src[p0:p1, lo - by:hi - by],
                                                 src[p0:p1, lo + by:hi + by], ALU.add))

            def pooling(i):
                whole = [(0, P)]
                step(nc.vector.tensor_tensor(X[:, 1:], U[:, 0:S + 2 * PAD - 1], U[:, 1:], ALU.add))
                if i == 0:
                    double(Y, X, 1, 2, [(96, P)])
                    parts = [(0, 96, X), (96, P, Y)]
                elif i == 1:
                    double(Y, X, 1, 2, whole)
                    double(X, Y, 2, 4, [(64, P)])
                    parts = [(0, 64, Y), (64, P, X)]
                else:
                    double(Y, X, 1, 2, whole)
                    double(X, Y, 2, 4, whole)
                    double(Y, X, 4, 8, [(32, 64), (64, P)])
                    parts = [(0, 32, X), (32, 64, Y), (64, P, Y)]
                for p0, p1, w in parts:
                    inner = slice(2 * PAD, S)
                    step(nc.vector.scalar_tensor_tensor(
                        out=U[p0:p1, inner], in0=w[p0:p1, inner], scalar=invw[p0:p1, i:i + 1],
                        in1=U[p0:p1, inner], op0=ALU.mult, op1=ALU.subtract))
                    for e, c0 in enumerate((PAD, S)):
                        ed = edge[p0:p1, e * PAD:(e + 1) * PAD]
                        step(nc.vector.tensor_tensor(ed, w[p0:p1, c0:c0 + PAD],
                                                     invcnt[p0:p1, i, e * PAD:(e + 1) * PAD], ALU.mult))
                        step(nc.vector.tensor_tensor(U[p0:p1, c0:c0 + PAD], ed, U[p0:p1, c0:c0 + PAD],
                                                     ALU.subtract))
                nc.vector.tensor_copy(edge[:, 0:1], edge[:, 1:2]).then_inc(pool_done, 1)

            split_w(0)
            for k in range(14):
                if k + 1 < 14:
                    split_w(k + 1)
                if 2 <= k < 5:
                    dve.wait_ge(act_ev, NB * (k + 1))
                    pooling(k - 2)
                elif k >= 5:
                    q, r = divmod(k - 5, 3)
                    if r == 1:
                        if q == 0:
                            dve.wait_ge(st_u, 16 * CT)
                        dve.wait_ge(act_ev, NB * (6 + 2 * q))
                        for b in range(NB):
                            blk = slice(PAD + b * 512, PAD + (b + 1) * 512)
                            dve.wait_ge(z_mm, NB * k + b + 1)
                            nc.vector.tensor_tensor(U[:, blk], ps[:, 4 + b, :], X[:, blk], ALU.mult
                                                    ).then_inc(dve_ev, 1)
                    elif r == 2:
                        dve.wait_ge(tap0, q + 1)
                        dve.wait_ge(dve_ev, NB * (q + 1))
                        nc.vector.scalar_tensor_tensor(out=X[:, core], in0=U[:, core],
                                                       scalar=wconv[:, q, 1:2], in1=X[:, core],
                                                       op0=ALU.mult, op1=ALU.add).then_inc(tap1, 1)
                        dve.wait_ge(tap1, q + 1)
                        nc.vector.scalar_tensor_tensor(out=X[:, core], in0=U[:, PAD + 1:PAD + 1 + S],
                                                       scalar=wconv[:, q, 2:3], in1=X[:, core],
                                                       op0=ALU.mult, op1=ALU.add).then_inc(tap2, 1)
                        dve.wait_ge(tap2, q + 1)
                        dve.wait_ge(act_ev, NB * (7 + 2 * q))
                        nc.vector.tensor_tensor(X[:, core], X[:, core], Y[:, core], ALU.mult
                                                ).then_inc(conv_done, 1)

        @block.tensor
        def _(pe):
            def transposes(n, s):
                pe.wait_ge(xn_done, n + 1)
                if not isinstance(n, int) or n >= 2:
                    pe.wait_ge(xlo_done, n - 1)
                for k in range(KT):
                    ins = nc.tensor.transpose(ps[:, 2 * s + k // 4, (k % 4) * P:(k % 4 + 1) * P],
                                              xn[:, s, k * P:(k + 1) * P], ident[:, :])
                ins.then_inc(tr_done, 1)

            pe.wait_ge(const_ld, 80)
            transposes(0, 0)
            transposes(1, 1)
            with pe.Fori(1, TILES // 2) as i:
                for s in range(2):
                    transposes(2 * i + s, s)
            pe.wait_ge(xlo_done, TILES)

            for k in range(14):
                pe.wait_ge(wlo_done, k + 1)
                for b in range(NB):
                    if k >= 1:
                        q, r = divmod(k - 6, 3)
                        if k >= 7 and r == 1:
                            pe.wait_ge(dve_ev, NB * q + b + 1)
                        else:
                            n_act = k if k < 7 else k - (q if r < 1 else q + 1)
                            pe.wait_ge(act_ev, NB * (n_act - 1) + b + 1)
                    blk = slice(b * 512, (b + 1) * 512)
                    mm3(nc, ps[:, 4 + b, :],
                        [((w_hi[:, k % 3, c, :], w_lo[:, k % 3, c, :]),
                          (xT_hi[:, c, blk], xT_lo[:, c, blk])) for c in range(KT)]).then_inc(z_mm, 1)


def stage_b(nc, t, ps, uf, y):
    MB = P // 4
    tw_v = t["tw"]
    uf_v = uf[:, :, :].rearrange("p c (n r) -> p r c n", r=R1)
    CH = 8

    with Alloc(nc) as m:
        dft = m.sb("dft", [P, 2, P])
        wf = m.sb("wf", [P, FT, P])
        m_hi, m_lo = m.pair("m", [P, FT, 3 * P])
        us_hi, us_lo = m.pair("us", [P, 2, FT, P])
        tw = m.sb("tw_raw", [P, 2, 2, P])
        tw_hi, tw_lo = m.pair("tw", [P, 2, 2, P])
        ab_hi, ab_lo = m.pair("ab", [P, 2, FT, 3 * P])
        g = m.sb("g", [P, 2, FT * 2 * P])
        g3 = m.sb("g3", [P, FT, MB, P])
        g3_hi, g3_lo = m.pair("g3", [P, 2, CH * P])
        t16 = m.sb("t16_raw", [P, 64])
        t16_hi, t16_lo = m.pair("t16", [P, 64])
        wp = m.sb("wp_raw", [P, CT, CT * P])
        wp_hi, wp_lo = m.pair("wp", [P, CT, CT * P])
        pr = m.sb("pr", [P, 2, CT, 512])
        pr_hi, pr_lo = m.pair("pr", [P, CT, 512])
        pscale = m.sb("pscale", [P, CT])

        zeroed = m.sem("b_zeroed")
        c_ld = m.sem("b_c_ld")
        y_ld = m.sem("b_y_ld")
        tw_ld = [m.sem(f"b_tw_ld{i}") for i in range(2)]
        mix_mm = m.sem("b_mix_mm")
        mhi = m.sem("b_mhi")
        mlo = m.sem("b_mlo")
        prep_hi = m.sem("b_prep_hi")
        prep_lo = m.sem("b_prep_lo")
        f1_mm = m.sem("b_f1_mm")
        ab_h = m.sem("b_ab_h")
        ab_l = m.sem("b_ab_l")
        f2_mm = m.sem("b_f2_mm")
        g_ev = m.sem("b_g_ev")
        g_st = [m.sem(f"b_g_st{i}") for i in range(2)]
        pr_ld = [m.sem(f"b_pr_ld{i}") for i in range(2)]
        w2hi = m.sem("b_w2hi")
        w2lo = m.sem("b_w2lo")
        prh = m.sem("b_prh")
        prl = m.sem("b_prl")
        p_mm = m.sem("b_p_mm")
        p_ev = m.sem("b_p_ev")
        g3_ld = [m.sem(f"b_g3_ld{i}") for i in range(2)]
        g3h = m.sem("b_g3h")
        g3l = m.sem("b_g3l")
        f3_mm = m.sem("b_f3_mm")
        f3_ev = m.sem("b_f3_ev")

        block = m.block()
        pieces = [(j, r // P, r % P, r - 96 * j, n) for j in range(4)
                  for r, n in ([(0, 96)], [(96, 32), (128, 64)], [(192, 64), (256, 32)], [(288, 96)])[j]]
        NC = 3 + FT * 2 + len(pieces)

        @block.sync
        def _(sp):
            sp.dma_start(dft[:, :, :], t["dft64"]).then_inc(c_ld, 16)
            sp.wait_ge(zeroed, 2)
            for h in range(2 * FT):
                sp.dma_start(wf[64 * (h % 2):64 * (h % 2) + 64, h // 2, 64 * (h % 2):64 * (h % 2) + 64],
                             t["w_fourier"][0, h, :, :]).then_inc(c_ld, 16)
            for n in range(2):
                sp.dma_start(tw[:, n, :, :], tw_v[:, n, :, :]).then_inc(tw_ld[n], 16)
            sp.dma_start(t16[:, :], t["t16"]).then_inc(c_ld, 16)
            sp.dma_start(pscale[:, :], t["pscale"]).then_inc(c_ld, 16)
            for j, tile, p0, r0, n in pieces:
                sp.dma_start(wp[p0:p0 + n, tile, 96 * j:96 * j + 96], t["w_pool"][0, j, r0:r0 + n, :]
                             ).then_inc(c_ld, 16)
            for b in range(2):
                sp.dma_start(pr[:, b, :, :], t["pooled"][:, :, b * 512:(b + 1) * 512]).then_inc(pr_ld[b], 16)
            for e in range(2):
                sp.dma_start(y[e][:, 0:CT, :], t["yconv"][:, :, e * HS:(e + 1) * HS]).then_inc(y_ld, 16)

            def g_store(n, s):
                sp.wait_ge(g_ev, n + 1)
                sp.dma_start(t["g"][:, :, bass.ds(n, 1), :].rearrange("c k o x -> k c (o x)"),
                             g[:, s, :].rearrange("p (c x) -> p c x", c=FT)).then_inc(g_st[s], 16)

            with sp.Fori(0, R1 // 2 - 1) as i:
                for s in range(2):
                    sp.wait_ge(prep_lo, 2 * i + s + 1)
                    sp.dma_start(tw[:, s, :, :], tw_v[:, bass.ds(2 * i + s + 2, 1), :, :].rearrange(
                        "p o a b -> p (o a) b")).then_inc(tw_ld[s], 16)
                for s in range(2):
                    g_store(2 * i + s, s)
            for s in range(2):
                g_store(R1 - 2 + s, s)
            for s in range(2):
                sp.wait_ge(g_st[s], 16 * R1 // 2)
            for c in range(FT):
                for a in range(4):
                    sp.dma_start(g3[32 * a:32 * a + 32, c, :, :],
                                 t["g"][c, 32 * a:32 * a + 32, :, :].rearrange(
                                     "b n (i x) -> (n i) b x", i=2)).then_inc(g3_ld[c], 16)
            for b in range(2, NB):
                sp.wait_ge(prl, b - 1)
                sp.dma_start(pr[:, b % 2, :, :], t["pooled"][:, :, b * 512:(b + 1) * 512]
                             ).then_inc(pr_ld[b % 2], 16)
            sp.wait_ge(y_ld, 32)

        @block.gpsimd
        def _(pool):
            nc.gpsimd.memset(wf[:, :, :], 0.0).then_inc(zeroed, 1)
            nc.gpsimd.memset(wp[:, :, :], 0.0).then_inc(zeroed, 1)

        @block.scalar
        def _(act):
            act.wait_ge(mix_mm, 1)
            for c in range(FT):
                nc.scalar.activation(m_hi[:, c, P:3 * P], ps[:, c, 0:2 * P], ACT.Copy)
                ins = nc.scalar.activation(m_hi[:, c, 0:P], ps[:, c, P:2 * P], ACT.Copy, scale=-1.0)
            ins.then_inc(mhi, 1)

            def prep(n, s, i=0):
                act.wait_ge(tw_ld[s], 16 * (i + 1))
                if not (isinstance(n, int) and n < 2):
                    act.wait_ge(f2_mm, n - 1)
                nc.scalar.activation(us_hi[:, s, :, :], uf_v[:, bass.ds(n, 1), :, :].rearrange(
                    "p o c n -> p (o c) n"), ACT.Copy)
                nc.scalar.activation(tw_hi[:, s, :, :], tw[:, s, :, :], ACT.Copy).then_inc(prep_hi, 1)

            def ab(n, s):
                act.wait_ge(f1_mm, n + 1)
                for c in range(FT):
                    ins = nc.scalar.activation(ab_hi[:, s, c, :], ps[:, 2 * s + c, 0:3 * P], ACT.Copy)
                ins.then_inc(ab_h, 1)

            prep(0, 0)
            prep(1, 1)
            with act.Fori(0, R1 // 2 - 1) as i:
                for s in range(2):
                    ab(2 * i + s, s)
                    prep(2 * i + 2 + s, s, i + 1)
            ab(R1 - 2, 0)
            ab(R1 - 1, 1)

            act.wait_ge(c_ld, 16 * NC)
            nc.scalar.activation(wp_hi[:, :, :], wp[:, :, :], ACT.Copy)
            nc.scalar.activation(t16_hi[:, :], t16[:, :], ACT.Copy).then_inc(w2hi, 1)

            def pr_split(b):
                act.wait_ge(pr_ld[b % 2], 16 * (b // 2 + 1))
                if b >= 1:
                    act.wait_ge(p_mm, CT * b)
                nc.scalar.activation(pr_hi[:, :, :], pr[:, b % 2, :, :], ACT.Copy).then_inc(prh, 1)

            for b in range(NB):
                pr_split(b)
                for o in range(CT):
                    act.wait_ge(p_mm, CT * b + o + 1)
                    nc.scalar.activation(y[b // 2][:, CT + FT + o, b % 2 * 512:b % 2 * 512 + 512], ps[:, 5 + o, :], ACT.Copy,
                                         scale=pscale[:, o:o + 1]).then_inc(p_ev, 1)

            def g3_split(j):
                if j % 4 == 0:
                    act.wait_ge(g3_ld[j // 4], 64)
                if j >= 2:
                    act.wait_ge(f3_mm, j - 1)
                nc.scalar.activation(g3_hi[:, j % 2, :], g3[:, j // 4, (j % 4) * CH:(j % 4 + 1) * CH, :
                                                            ].rearrange("p b x -> p (b x)"), ACT.Copy
                                     ).then_inc(g3h, 1)

            g3_split(0)
            g3_split(1)
            for j in range(4 * FT):
                act.wait_ge(f3_mm, j + 1)
                for e in range(2):
                    out = y[e][:, CT + j // 4, :].rearrange("p (m b) -> p b m", b=MB)
                    ins = nc.scalar.activation(
                        out[:, (j % 4) * CH:(j % 4 + 1) * CH, :],
                        ps[:, j % 4, :].rearrange("p (b e m) -> p e b m", b=CH, e=2)[:, e, :, :], ACT.Copy)
                ins.then_inc(f3_ev, 1)
                if j + 2 < 4 * FT:
                    g3_split(j + 2)

        @block.vector
        def _(dve):
            dve.wait_ge(mhi, 1)
            for c in range(FT):
                split_lo(nc, m_lo[:, c, P:3 * P], ps[:, c, 0:2 * P], m_hi[:, c, P:3 * P])
                ins = nc.vector.scalar_tensor_tensor(out=m_lo[:, c, 0:P], in0=ps[:, c, P:2 * P], scalar=-1.0,
                                                     in1=m_hi[:, c, 0:P].bitcast(F32), op0=ALU.mult,
                                                     op1=ALU.subtract)
            ins.then_inc(mlo, 1)

            def prep(n, s):
                dve.wait_ge(prep_hi, n + 1)
                split_lo(nc, us_lo[:, s, :, :], uf_v[:, bass.ds(n, 1), :, :].rearrange("p o c n -> p (o c) n"),
                         us_hi[:, s, :, :])
                split_lo(nc, tw_lo[:, s, :, :], tw[:, s, :, :], tw_hi[:, s, :, :]).then_inc(prep_lo, 1)

            def ab(n, s):
                dve.wait_ge(ab_h, n + 1)
                for c in range(FT):
                    ins = split_lo(nc, ab_lo[:, s, c, :], ps[:, 2 * s + c, 0:3 * P], ab_hi[:, s, c, :])
                ins.then_inc(ab_l, 1)

            def g_out(n, s, i=0):
                dve.wait_ge(f2_mm, n + 1)
                if not (isinstance(n, int) and n < 2):
                    dve.wait_ge(g_st[s], 16 * i)
                nc.vector.tensor_copy(g[:, s, :], ps[:, 4 + s, :]).then_inc(g_ev, 1)

            prep(0, 0)
            prep(1, 1)
            ab(0, 0)
            ab(1, 1)
            g_out(0, 0)
            g_out(1, 1)
            with dve.Fori(1, R1 // 2) as i:
                for s in range(2):
                    prep(2 * i + s, s)
                for s in range(2):
                    ab(2 * i + s, s)
                for s in range(2):
                    g_out(2 * i + s, s, i)

            dve.wait_ge(w2hi, 1)
            split_lo(nc, wp_lo[:, :, :], wp[:, :, :], wp_hi[:, :, :])
            split_lo(nc, t16_lo[:, :], t16[:, :], t16_hi[:, :]).then_inc(w2lo, 1)
            for b in range(NB):
                dve.wait_ge(prh, b + 1)
                split_lo(nc, pr_lo[:, :, :], pr[:, b % 2, :, :], pr_hi[:, :, :]).then_inc(prl, 1)
            for j in range(4 * FT):
                dve.wait_ge(g3h, j + 1)
                split_lo(nc, g3_lo[:, j % 2, :], g3[:, j // 4, (j % 4) * CH:(j % 4 + 1) * CH, :].rearrange(
                    "p b x -> p (b x)"), g3_hi[:, j % 2, :]).then_inc(g3l, 1)

        @block.tensor
        def _(pe):
            pe.wait_ge(c_ld, 16 * NC)
            for c in range(FT):
                for f in range(2):
                    ins = nc.tensor.matmul(ps[:, c, f * P:(f + 1) * P], dft[:, f, :], wf[:, c, :],
                                           start=True, stop=True)
            ins.then_inc(mix_mm, 1)
            pe.wait_ge(mlo, 1)

            def f1(n, s):
                pe.wait_ge(prep_lo, n + 1)
                if not (isinstance(n, int) and n < 2):
                    pe.wait_ge(ab_l, n - 1)
                for c in range(FT):
                    ins = mm3(nc, ps[:, 2 * s + c, 0:3 * P],
                              [((us_hi[:, s, c, :], us_lo[:, s, c, :]), (m_hi[:, c, :], m_lo[:, c, :]))])
                ins.then_inc(f1_mm, 1)

            def f2(n, s):
                pe.wait_ge(ab_l, n + 1)
                if not (isinstance(n, int) and n < 2):
                    pe.wait_ge(g_ev, n - 1)
                terms = [((tw_hi[:, s, f, :], tw_lo[:, s, f, :]),
                          (ab_hi[:, s, :, P - f * P:3 * P - f * P], ab_lo[:, s, :, P - f * P:3 * P - f * P]))
                         for f in range(2)]
                mm3(nc, ps[:, 4 + s, :].rearrange("p (c x) -> p c x", c=FT), terms).then_inc(f2_mm, 1)

            f1(0, 0)
            f1(1, 1)
            f2(0, 0)
            f2(1, 1)
            f1(2, 0)
            f1(3, 1)
            with pe.Fori(1, R1 // 2 - 1) as i:
                for s in range(2):
                    f2(2 * i + s, s)
                for s in range(2):
                    f1(2 * i + 2 + s, s)
            f2(R1 - 2, 0)
            f2(R1 - 1, 1)

            pe.wait_ge(w2lo, 1)
            for b in range(NB):
                pe.wait_ge(prl, b + 1)
                for o, tiles in enumerate(((0, 1), (0, 1, 2), (1, 2))):
                    if b >= 1:
                        pe.wait_ge(p_ev, CT * (b - 1) + o + 1)
                    elif o == 0:
                        pe.wait_ge(g_ev, R1)
                    mm3(nc, ps[:, 5 + o, :],
                        [((wp_hi[:, i, o * P:(o + 1) * P], wp_lo[:, i, o * P:(o + 1) * P]),
                          (pr_hi[:, i, :], pr_lo[:, i, :])) for i in tiles]).then_inc(p_mm, 1)

            for j in range(4 * FT):
                pe.wait_ge(g3l, j + 1)
                if j >= 4:
                    pe.wait_ge(f3_ev, j - 3)
                for b in range(CH):
                    ins = mm3(nc, ps[:, j % 4, b * 64:(b + 1) * 64],
                              [((g3_hi[:, j % 2, b * P:(b + 1) * P], g3_lo[:, j % 2, b * P:(b + 1) * P]),
                                (t16_hi[:, :], t16_lo[:, :]))])
                ins.then_inc(f3_mm, 1)


def stage_cd(nc, t, ident, ps, m, y, free_y):
    x_v = t["x"].rearrange("o (n p) d -> (o n) p d", p=P)
    xm_v = t["xmid"]
    wo_v = t["w_out"].rearrange("o (k p) d -> (o k) p d", p=P)
    w13_v = [t[w].rearrange("o (k p) f -> p (o k) f", p=P) for w in ("w1", "w3")]
    w2_v = t["w2"].rearrange("o (j p) d -> p (o j) d", p=P)
    HT = TILES // 2
    FW = GF * P
    XC = KT // 2
    UB = GF
    DB = 8
    LAST = 2 * GROUPS

    w13_raw = m.sb("w13_raw", [P, 2, KT, FW], side="right")
    raw = m.sb("raw", [P, 2, D], side="right")
    consts = m.sb("cconsts", [P, 2], side="right")
    ss = m.sb("css", [P, 2], side="right")
    rstd = m.sb("crstd", [P, 2], side="right")
    with Alloc(nc) as mc:
        wo_hi, wo_lo = mc.pair("wo", [P, KT, D])
        ys_hi, ys_lo = mc.pair("ys", [P, 2, KT, P])
        x_in = mc.sb("cx_in", [P, 2, D])
        xm = mc.sb("xm", [P, 2, D])
        xn = mc.sb("cxn", [P, 2, D])
        xt = mc.sb("xt", [P, 2, KT, P])
        g_b = mc.sb("cg_b", [P, D])
    free_y()
    xf = [m.pair(f"xf{b}", [P, KT, 512]) for b in range(2)]
    w13_hi, w13_lo = m.pair("w13", [P, GF, 2, KT, P])
    w2_raw = m.sb("w2_raw", [P, GF, D])
    w2_hi, w2_lo = m.pair("w2", [P, GF, D])
    h_hi, h_lo = m.pair("h", [P, 2, GF, 512])
    sil = m.sb("sil", [P, GF, 512])
    hf = m.sb("hf", [P, GF, 512])
    acc = m.sb("acc", [P, HT, D])
    junk = m.sb("junk", [P, D], mybir.dt.bfloat16)
    gf_b = m.sb("gf_b", [P, D])

    g_ld = m.sem("c_g_ld")
    wo_ld = [m.sem(f"c_wo_ld{i}") for i in range(2)]
    wo_h = m.sem("c_wo_h")
    wo_l = m.sem("c_wo_l")
    x_ld = [m.sem(f"c_x_ld{i}") for i in range(2)]
    ys_h = m.sem("c_ys_h")
    ys_l = m.sem("c_ys_l")
    o_mm = m.sem("c_o_mm")
    xm_done = m.sem("c_xm_done")
    consts_set = m.sem("c_consts_set")
    sq_done = m.sem("c_sq_done")
    ms_done = m.sem("c_ms_done")
    rstd_done = m.sem("c_rstd_done")
    xn_done = m.sem("c_xn_done")
    tr_done = m.sem("c_tr_done")
    xt_done = m.sem("c_xt_done")
    xm_st = [m.sem(f"c_xm_st{i}") for i in range(2)]
    xt_st = [m.sem(f"c_xt_st{i}") for i in range(2)]

    xf_ld = [m.sem(f"d_xf_ld{i}") for i in range(2)]
    xfh = m.sem("d_xfh")
    xfl = m.sem("d_xfl")
    w13_ld = [m.sem(f"d_w{i}_ld") for i in (1, 3)]
    w13h = m.sem("d_w13h")
    w13l = m.sem("d_w13l")
    w2_ld = m.sem("d_w2_ld")
    w2h = m.sem("d_w2h")
    w2l = m.sem("d_w2l")
    up_mm = m.sem("d_up_mm")
    sil_done = m.sem("d_sil_done")
    hf_done = m.sem("d_hf_done")
    hh = m.sem("d_hh")
    hl = m.sem("d_hl")
    dn_mm = m.sem("d_dn_mm")
    acc_ld = [[m.sem(f"d_acc_ld{p}{b}") for b in range(2)] for p in range(2)]
    acc_done = m.sem("d_acc_done")
    gf_ld = m.sem("d_gf_ld")
    fsq = m.sem("d_fsq")
    fms = m.sem("d_fms")
    frs = m.sem("d_frs")
    o_done = m.sem("d_o_done")
    o_st = [[m.sem(f"d_o_st{p}{b}") for b in range(2)] for p in range(2)]

    block = m.block()

    def later(n):
        return not (isinstance(n, int) and n < 2)

    def rest(g):
        return not isinstance(g, int) or g > 0

    @block.sync
    def _(sp):
        for k in range(KT):
            if k >= 2:
                sp.wait_ge(wo_l, k - 1)
            sp.dma_start(raw[:, k % 2, :], wo_v[k, :, :]).then_inc(wo_ld[k % 2], 16)
            if k == 1:
                sp.dma_start(g_b[:, :], t["g_ffn"].to_broadcast([P, D])).then_inc(g_ld, 16)

        def x_load(n, s):
            if later(n):
                sp.wait_ge(xm_done, 2 * n - 2)
            sp.dma_start(x_in[:, s, :], x_v[bass.ds(n, 1), :, :].rearrange("o p d -> p (o d)")
                         ).then_inc(x_ld[s], 16)

        def store(n, s):
            sp.wait_ge(xm_done, 2 * n + 2)
            sp.dma_start(xm_v[bass.ds(n, 1), :, :].rearrange("o p d -> p (o d)"), xm[:, s, :]
                         ).then_inc(xm_st[s], 16)
            sp.wait_ge(xt_done, n + 1)
            sp.dma_start(t["xt"][:, :, bass.ds(n * P, P)], xt[:, s, :, :]).then_inc(xt_st[s], 16)

        def load13(i):
            for w in range(2):
                sp.dma_start(w13_raw[:, w, :, :], w13_v[w][:, :, bass.ds(i * FW, FW)]
                             ).then_inc(w13_ld[w], 16)

        def load2(i):
            sp.dma_start(w2_raw[:, :, :], w2_v[:, bass.ds(i * GF, GF), :]).then_inc(w2_ld, 16)

        def load_xf(part, b, k):
            c = (2 * part + b) * XC + k
            if c >= 2:
                sp.wait_ge(xfl, c - 1)
            sp.dma_start(raw[:, c % 2, :].rearrange("p (k t) -> p k t", k=2),
                         t["xt"][:, 2 * k:2 * k + 2, (2 * part + b) * 512:(2 * part + b + 1) * 512]
                         ).then_inc(xf_ld[c % 2], 16)

        def load_acc(part, b):
            n0 = part * HT + 4 * b
            sp.dma_start(acc[:, 4 * b:4 * b + 4, :], xm_v[n0:n0 + 4, :, :].rearrange("n p d -> p n d")
                         ).then_inc(acc_ld[part][b], 16)

        def store_out(part, b):
            for n in range(part * HT + 4 * b, part * HT + 4 * b + 4):
                sp.wait_ge(o_done, n + 1)
                sp.dma_start(t["out"][0, n * P:(n + 1) * P, :], acc[:, n % HT, :]).then_inc(o_st[part][b], 16)

        x_load(0, 0)
        x_load(1, 1)
        load13(0)
        with sp.Fori(0, TILES // 2 - 1) as i:
            for s in range(2):
                store(2 * i + s, s)
                x_load(2 * i + 2 + s, s)
        for s in range(2):
            sp.wait_ge(xt_st[s], 16 * (HT // 2))
            sp.wait_ge(xm_st[s], 16 * (HT // 2))
        sp.wait_ge(wo_l, KT)
        for k in range(XC):
            load_xf(0, 0, k)
        for s in range(2):
            load_xf(0, 1, 2 * s)
            load_xf(0, 1, 2 * s + 1)
            store(TILES - 2 + s, s)
        sp.wait_ge(tr_done, TILES)
        for s in range(2):
            sp.wait_ge(xm_st[s], 16 * HT)
            sp.wait_ge(xt_st[s], 16 * HT)
        load2(0)
        for b in range(2):
            load_acc(0, b)
        sp.dma_start(gf_b[:, :], t["g_final"].to_broadcast([P, D])).then_inc(gf_ld, 16)

        def loads(g, i):
            sp.wait_ge(w13l, 2 * GF * g)
            load13(i)
            sp.wait_ge(w2l, g)
            load2(i)

        with sp.Fori(1, GROUPS) as i:
            loads(i, i)
        sp.wait_ge(w13l, 2 * GF * GROUPS)
        load13(0)
        for k in range(XC):
            load_xf(1, 0, k)
        sp.wait_ge(w2l, GROUPS)
        load2(0)
        for k in range(XC):
            load_xf(1, 1, k)
        for b in range(2):
            store_out(0, b)
            sp.wait_ge(o_st[0][b], 16 * 4)
            load_acc(1, b)
        with sp.Fori(1, GROUPS) as i:
            loads(GROUPS + i, i)
        for b in range(2):
            store_out(1, b)
        for b in range(2):
            sp.wait_ge(o_st[1][b], 16 * 4)

    @block.gpsimd
    def _(pool):
        nc.gpsimd.memset(consts[:, 0:1], -0.5)
        nc.gpsimd.memset(consts[:, 1:2], EPS).then_inc(consts_set, 1)
        pool.wait_ge(consts_set, 1)

        def rms(n, s, squares, mean, root):
            pool.wait_ge(squares, n + 1)
            nc.gpsimd.tensor_tensor(ss[:, s:s + 1], ss[:, s:s + 1], consts[:, 1:2], ALU.add
                                    ).then_inc(mean, 1)
            pool.wait_ge(mean, n + 1)
            nc.gpsimd.tensor_tensor(rstd[:, s:s + 1], ss[:, s:s + 1], consts[:, 0:1], ALU.pow
                                    ).then_inc(root, 1)

        with pool.Fori(0, TILES // 2) as i:
            for s in range(2):
                rms(2 * i + s, s, sq_done, ms_done, rstd_done)
        for s in range(2):
            rms(s, s, fsq, fms, frs)
        with pool.Fori(1, TILES // 2) as i:
            for s in range(2):
                pool.wait_ge(o_done, 2 * i + s - 1)
                rms(2 * i + s, s, fsq, fms, frs)

    @block.scalar
    def _(act):
        for k in range(KT):
            act.wait_ge(wo_ld[k % 2], 16 * (k // 2 + 1))
            nc.scalar.activation(wo_hi[:, k, :], raw[:, k % 2, :], ACT.Copy).then_inc(wo_h, 1)

        def ys(n, s, part):
            if later(n):
                act.wait_ge(o_mm, 2 * n - 2)
            col = n * P - part * HS
            nc.scalar.activation(ys_hi[:, s, :, :], y[part][:, :, bass.ds(col, P)], ACT.Copy
                                 ).then_inc(ys_h, 1)

        def square(n, s):
            act.wait_ge(xm_done, 2 * n + 2)
            if later(n):
                act.wait_ge(tr_done, n - 1)
            nc.scalar.activation(xn[:, s, :], xm[:, s, :], ACT.Square, scale=D ** -0.5,
                                 accum_out=ss[:, s:s + 1]).then_inc(sq_done, 1)

        def evac(n, s, i=0):
            act.wait_ge(tr_done, n + 1)
            if later(n):
                act.wait_ge(xt_st[s], 16 * i)
            for b in range(2):
                ins = nc.scalar.activation(xt[:, s, 4 * b:4 * b + 4, :].rearrange("p k t -> p (k t)"),
                                           ps[:, 4 + 2 * s + b, :], ACT.Copy)
            ins.then_inc(xt_done, 1)

        def xf_split(part, b, k):
            c = (2 * part + b) * XC + k
            act.wait_ge(xf_ld[c % 2], 16 * (c // 2 + 1))
            if part and k == 0:
                act.wait_ge(up_mm, 2 * UB * (GROUPS - 1) + UB * (b + 1))
            nc.scalar.activation(xf[b][0][:, 2 * k:2 * k + 2, :],
                                 raw[:, c % 2, :].rearrange("p (k t) -> p k t", k=2), ACT.Copy
                                 ).then_inc(xfh, 1)

        ys(0, 0, 0)
        ys(1, 1, 0)
        for s in range(2):
            ys(2 + s, s, 0)
            square(s, s)
            evac(s, s)
        for part, (a, b) in enumerate(((1, HT // 2 - 1), (HT // 2 - 1, TILES // 2 - 1))):
            with act.Fori(a, b) as i:
                for s in range(2):
                    ys(2 * i + 2 + s, s, part)
                    square(2 * i + s, s)
                    evac(2 * i + s, s, i)
        act.wait_ge(ys_l, HT)
        for k in range(XC):
            xf_split(0, 0, k)
        for s in range(2):
            square(TILES - 2 + s, s)
            if s == 0:
                evac(TILES - 2, 0, HT - 1)

        def w13_split(g, f):
            for w in range(2):
                act.wait_ge(w13_ld[w], 16 * g + 16)
            if rest(g):
                act.wait_ge(up_mm, 2 * UB * g - UB + f + 1)
            for w in range(2):
                nc.scalar.activation(w13_hi[:, f, w, :, :], w13_raw[:, w, :, f * P:(f + 1) * P],
                                     ACT.Copy).then_inc(w13h, 1)

        def w2_split(g):
            act.wait_ge(w2_ld, 16 * g + 16)
            if rest(g):
                act.wait_ge(dn_mm, 2 * DB * g)
            nc.scalar.activation(w2_hi[:, :, :], w2_raw[:, :, :], ACT.Copy).then_inc(w2h, 1)

        def activate(g, b, f):
            n = 2 * UB * g + UB * b + f
            act.wait_ge(up_mm, n + 1)
            if not isinstance(g, int) or n >= GF:
                act.wait_ge(hf_done, n - 1)
            nc.scalar.activation(sil[:, f, :], ps[:, 2 * f, :], ACT.Silu).then_inc(sil_done, 1)
            act.wait_ge(hf_done, n + 1)
            nc.scalar.activation(h_hi[:, b, f, :], hf[:, f, :], ACT.Copy).then_inc(hh, 1)

        def final_square(part, b):
            for j in range(4):
                n = part * HT + 4 * b + j
                act.wait_ge(acc_done, 2 * DB * (GROUPS * (part + 1) - 1) + DB * b + 2 * j + 2)
                if n >= 1:
                    act.wait_ge(fsq, n)
                if n >= 2:
                    act.wait_ge(frs, n - 1)
                nc.scalar.activation(junk[:, :], acc[:, 4 * b + j, :], ACT.Square, scale=D ** -0.5,
                                     accum_out=ss[:, n % 2:n % 2 + 1]).then_inc(fsq, 1)

        act.wait_ge(o_mm, 2 * TILES)
        w13_split(0, 0)
        w13_split(0, 1)
        evac(TILES - 1, 1, HT - 1)
        act.wait_ge(tr_done, TILES)
        for k in range(XC):
            xf_split(0, 1, k)
        w2_split(0)
        for f in range(GF):
            activate(0, 0, f)

        def group(g, more):
            for f in range(GF):
                activate(g, 1, f)
                if more:
                    w13_split(g + 1, f)
            if more:
                for f in range(GF):
                    activate(g + 1, 0, f)
                w2_split(g + 1)

        with act.Fori(0, GROUPS - 1) as i:
            group(i, True)
        g = GROUPS - 1
        for k in range(XC):
            xf_split(1, 0, k)
        for f in range(GF):
            activate(g, 1, f)
            w13_split(g + 1, f)
        for k in range(XC):
            xf_split(1, 1, k)
        final_square(0, 0)
        for f in range(GF):
            activate(g + 1, 0, f)
        w2_split(g + 1)
        final_square(0, 1)
        with act.Fori(GROUPS, LAST - 1) as i:
            group(i, True)
        group(LAST - 1, False)
        final_square(1, 0)
        final_square(1, 1)

    @block.vector
    def _(dve):
        for k in range(KT):
            dve.wait_ge(wo_h, k + 1)
            split_lo(nc, wo_lo[:, k, :], raw[:, k % 2, :], wo_hi[:, k, :]).then_inc(wo_l, 1)
        dve.wait_ge(g_ld, 16)

        def ys(n, s, part):
            dve.wait_ge(ys_h, n + 1)
            col = n * P - part * HS
            split_lo(nc, ys_lo[:, s, :, :], y[part][:, :, bass.ds(col, P)], ys_hi[:, s, :, :]
                     ).then_inc(ys_l, 1)

        def residual(n, s, i=0):
            dve.wait_ge(x_ld[s], 16 * (i + 1))
            if later(n):
                dve.wait_ge(xm_st[s], 16 * i)
                dve.wait_ge(xn_done, n - 1)
            for b in range(2):
                dve.wait_ge(o_mm, 2 * n + b + 1)
                nc.vector.tensor_tensor(xm[:, s, b * 512:(b + 1) * 512], ps[:, 2 * s + b, :],
                                        x_in[:, s, b * 512:(b + 1) * 512], ALU.add
                                        ).then_inc(xm_done, 1)

        def norm(n, s):
            dve.wait_ge(rstd_done, n + 1)
            nc.vector.scalar_tensor_tensor(out=xn[:, s, :], in0=xm[:, s, :],
                                           scalar=rstd[:, s:s + 1], in1=g_b[:, :], op0=ALU.mult,
                                           op1=ALU.mult).then_inc(xn_done, 1)

        def xf_split(part, b, k):
            c = (2 * part + b) * XC + k
            dve.wait_ge(xfh, c + 1)
            split_lo(nc, xf[b][1][:, 2 * k:2 * k + 2, :], raw[:, c % 2, :].rearrange("p (k t) -> p k t", k=2),
                     xf[b][0][:, 2 * k:2 * k + 2, :]).then_inc(xfl, 1)

        ys(0, 0, 0)
        ys(1, 1, 0)
        for s in range(2):
            residual(s, s)
            ys(2 + s, s, 0)
            norm(s, s)
        for part, (a, b) in enumerate(((1, HT // 2 - 1), (HT // 2 - 1, TILES // 2 - 1))):
            with dve.Fori(a, b) as i:
                for s in range(2):
                    residual(2 * i + s, s, i)
                    ys(2 * i + 2 + s, s, part)
                    norm(2 * i + s, s)
        for k in range(XC):
            xf_split(0, 0, k)
        for s in range(2):
            residual(TILES - 2 + s, s, HT - 1)
            if s == 0:
                norm(TILES - 2, 0)

        def w13_split(g, f):
            for w in range(2):
                dve.wait_ge(w13h, 2 * GF * g + 2 * f + w + 1)
                split_lo(nc, w13_lo[:, f, w, :, :], w13_raw[:, w, :, f * P:(f + 1) * P],
                         w13_hi[:, f, w, :, :]).then_inc(w13l, 1)

        def w2_split(g):
            dve.wait_ge(w2h, g + 1)
            split_lo(nc, w2_lo[:, :, :], w2_raw[:, :, :], w2_hi[:, :, :]).then_inc(w2l, 1)

        def activate(g, b, f):
            n = 2 * UB * g + UB * b + f
            dve.wait_ge(sil_done, n + 1)
            if not isinstance(g, int) or n >= GF:
                dve.wait_ge(hl, n - 1)
            nc.vector.tensor_tensor(hf[:, f, :], ps[:, 2 * f + 1, :], sil[:, f, :], ALU.mult
                                    ).then_inc(hf_done, 1)
            dve.wait_ge(hh, n + 1)
            split_lo(nc, h_lo[:, b, f, :], hf[:, f, :], h_hi[:, b, f, :]).then_inc(hl, 1)

        def add(g, b):
            for j in range(DB):
                n = 2 * DB * g + DB * b + j
                dve.wait_ge(dn_mm, n + 1)
                if isinstance(g, int) and g % GROUPS == 0:
                    if j == 0:
                        dve.wait_ge(acc_ld[g // GROUPS][b], 16)
                else:
                    dve.wait_ge(acc_done, n + 1 - 2 * DB)
                part_of = acc[:, 4 * b + j // 2, (j % 2) * 512:(j % 2 + 1) * 512]
                nc.vector.tensor_tensor(part_of, ps[:, 4 + j % 4, :], part_of, ALU.add
                                        ).then_inc(acc_done, 1)

        def final_norm(part, b):
            for j in range(4):
                n = part * HT + 4 * b + j
                dve.wait_ge(frs, n + 1)
                nc.vector.scalar_tensor_tensor(out=acc[:, 4 * b + j, :], in0=acc[:, 4 * b + j, :],
                                               scalar=rstd[:, n % 2:n % 2 + 1], in1=gf_b[:, :],
                                               op0=ALU.mult, op1=ALU.mult).then_inc(o_done, 1)

        dve.wait_ge(o_mm, 2 * TILES)
        w13_split(0, 0)
        norm(TILES - 1, 1)
        w13_split(0, 1)
        for k in range(XC):
            xf_split(0, 1, k)
        w2_split(0)
        for f in range(GF):
            activate(0, 0, f)

        def group(g, more):
            activate(g, 1, 0)
            if more:
                w13_split(g + 1, 0)
            activate(g, 1, 1)
            add(g, 0)
            if more:
                w13_split(g + 1, 1)
                for f in range(GF):
                    activate(g + 1, 0, f)
            add(g, 1)
            if more:
                w2_split(g + 1)

        group(0, True)
        with dve.Fori(1, GROUPS - 1) as i:
            group(i, True)
        g = GROUPS - 1
        for k in range(XC):
            xf_split(1, 0, k)
        activate(g, 1, 0)
        w13_split(g + 1, 0)
        activate(g, 1, 1)
        add(g, 0)
        w13_split(g + 1, 1)
        for k in range(XC):
            xf_split(1, 1, k)
        dve.wait_ge(gf_ld, 16)
        final_norm(0, 0)
        for f in range(GF):
            activate(g + 1, 0, f)
        add(g, 1)
        w2_split(g + 1)
        final_norm(0, 1)
        group(GROUPS, True)
        with dve.Fori(GROUPS + 1, LAST - 1) as i:
            group(i, True)
        g = LAST - 1
        activate(g, 1, 0)
        activate(g, 1, 1)
        add(g, 0)
        final_norm(1, 0)
        add(g, 1)
        final_norm(1, 1)

    @block.tensor
    def _(pe):
        pe.wait_ge(wo_l, KT)

        def products(n, s):
            pe.wait_ge(ys_l, n + 1)
            for b in range(2):
                if later(n):
                    pe.wait_ge(xm_done, 2 * (n - 2) + b + 1)
                mm3(nc, ps[:, 2 * s + b, :],
                    [((ys_hi[:, s, k, :], ys_lo[:, s, k, :]),
                      (wo_hi[:, k, b * 512:(b + 1) * 512], wo_lo[:, k, b * 512:(b + 1) * 512]))
                     for k in range(KT)]).then_inc(o_mm, 1)

        def transposes(n, s):
            pe.wait_ge(xn_done, n + 1)
            if later(n):
                pe.wait_ge(xt_done, n - 1)
            for k in range(KT):
                ins = nc.tensor.transpose(ps[:, 4 + 2 * s + k // 4, (k % 4) * P:(k % 4 + 1) * P],
                                          xn[:, s, k * P:(k + 1) * P], ident[:, :])
            ins.then_inc(tr_done, 1)

        products(0, 0)
        products(1, 1)
        transposes(0, 0)
        products(2, 0)
        transposes(1, 1)
        with pe.Fori(1, TILES // 2 - 1) as i:
            products(2 * i + 1, 1)
            transposes(2 * i, 0)
            products(2 * i + 2, 0)
            transposes(2 * i + 1, 1)
        products(TILES - 1, 1)
        transposes(TILES - 2, 0)

        def up(g, b):
            for f in range(GF):
                n = 2 * UB * g + UB * b + f
                for w in range(2):
                    if b == 0:
                        pe.wait_ge(w13l, 2 * GF * g + 2 * f + w + 1)
                    if not isinstance(g, int) or n >= GF:
                        pe.wait_ge((sil_done, hf_done)[w], n - 1)
                    elif n == 0 and w == 0:
                        pe.wait_ge(xm_done, 2 * TILES)
                    if isinstance(g, int) and g % GROUPS == 0 and f == 0 and w == 0:
                        pe.wait_ge(xfl, (2 * (g // GROUPS) + b + 1) * XC)
                    ins = mm3(nc, ps[:, 2 * f + w, :],
                              [((w13_hi[:, f, w, k, :], w13_lo[:, f, w, k, :]),
                                (xf[b][0][:, k, :], xf[b][1][:, k, :])) for k in range(KT)])
                    if isinstance(g, int) and n == 0 and w == 0:
                        transposes(TILES - 1, 1)
                ins.then_inc(up_mm, 1)

        def down(g, b):
            pe.wait_ge(hl, 2 * UB * g + UB * b + UB)
            if b == 0:
                pe.wait_ge(w2l, g + 1)
            for j in range(DB):
                n = 2 * DB * g + DB * b + j
                if not isinstance(g, int) or n >= 4:
                    pe.wait_ge(acc_done, n - 3)
                elif n == 0:
                    pe.wait_ge(xt_done, TILES)
                tok = slice((j // 2) * P, (j // 2 + 1) * P)
                col = slice((j % 2) * 512, (j % 2 + 1) * 512)
                mm3(nc, ps[:, 4 + j % 4, :],
                    [((h_hi[:, b, f, tok], h_lo[:, b, f, tok]), (w2_hi[:, f, col], w2_lo[:, f, col]))
                     for f in range(GF)]).then_inc(dn_mm, 1)

        def group(g):
            up(g, 1)
            down(g, 0)
            up(g + 1, 0)
            down(g, 1)

        up(0, 0)
        group(0)
        with pe.Fori(1, GROUPS - 1) as i:
            group(i)
        group(GROUPS - 1)
        group(GROUPS)
        with pe.Fori(GROUPS + 1, LAST - 1) as i:
            group(i)
        up(LAST - 1, 1)
        down(LAST - 1, 0)
        down(LAST - 1, 1)


def encoder_layer(nc, t):
    with Alloc(nc) as m:
        ident = m.sb("ident", [P, P])
        ps = m.stack.enter_context(nc.psum_tensor("ps", [P, 8, 512], F32))
        y_mem = Alloc(nc)
        with Alloc(nc) as mu:
            uf = mu.sb("uf", [P, FT, S], side="right")
            stage_a(nc, t, ident, ps, uf)
            y_mem.__enter__()
            y = [y_mem.sb(f"y{e}", [P, KT, HS]) for e in range(2)]
            stage_b(nc, t, ps, uf, y)
        with Alloc(nc) as md:
            stage_cd(nc, t, ident, ps, md, y, y_mem.stack.close)


def shape_constants():
    import numpy as np
    hd = 64
    j = np.arange(hd)
    ang = 2 * np.pi * np.outer(j, j) / hd
    norm = 1.0 / np.sqrt(S * hd)
    dft64 = np.zeros((P, 2, P))
    for f, mat in enumerate((np.cos(ang), np.sin(ang))):
        for h in range(2):
            dft64[hd * h:hd * h + hd, f, hd * h:hd * h + hd] = mat * norm
    n2 = np.arange(P)[:, None, None]
    n1 = np.arange(R1)[None, :, None]
    k2 = np.arange(P)[None, None, :]
    ang = 2 * np.pi * (((n1 + R1 * n2) * k2) % S) / S
    tw = np.stack([np.cos(ang), np.sin(ang)], axis=2)
    t16 = np.zeros((4, R1, 2, R1, 4))
    k1 = np.arange(R1)
    ang = 2 * np.pi * (np.outer(k1, k1) % R1) / R1
    for a in range(4):
        t16[a, :, 0, :, a] = np.cos(ang)
        t16[a, :, 1, :, a] = -np.sin(ang)
    windows = np.repeat([2, 4, 8, 16], 96)
    tok = np.concatenate([np.arange(PAD), np.arange(S - PAD, S)])
    cnt = (np.minimum(tok + windows[:, None] // 2, S) - np.maximum(tok - windows[:, None] // 2, 0))
    f = np.float32
    return {
        "ident": np.eye(P, dtype=f), "dft64": dft64.astype(f), "tw": tw.astype(f),
        "t16": t16.reshape(P, 64).astype(f),
        "invw": np.ascontiguousarray((1.0 / windows).reshape(CT, P).T).astype(f),
        "invcnt": np.ascontiguousarray((1.0 / cnt).reshape(CT, P, 2 * PAD).transpose(1, 0, 2)).astype(f),
    }


_INS = ["x", "g_mix", "w_in", "w_fourier", "w_pool", "w_out", "g_ffn", "w1", "w3", "w2"]


def kernel(**inputs):
    import numpy as np
    import concourse.bacc as bacc
    from concourse.bass_utils import run_bass_kernel_spmd

    nc = bacc.Bacc("TRN2", target_bir_lowering=False, num_devices=1)
    arrays = {n: np.ascontiguousarray(inputs[n]) for n in _INS}
    arrays["g_final"] = np.ascontiguousarray(inputs["g_final"]).reshape(1, D)
    arrays["wconv"] = np.ascontiguousarray(np.asarray(inputs["w_conv"]).reshape(3, CT, P).transpose(2, 1, 0))
    arrays["pscale"] = np.ascontiguousarray(np.asarray(inputs["pool_scale"]).reshape(CT, P).T)
    arrays.update(shape_constants())
    t = {n: nc.dram_tensor(f"in_{n}", a.shape, mybir.dt.from_np(a.dtype), kind="ExternalInput").ap()
         for n, a in arrays.items()}
    t["out"] = nc.dram_tensor("out", (1, S, D), F32, kind="ExternalOutput").ap()
    for n, shape in (("yconv", (P, CT, S)), ("pooled", (P, CT, S)), ("g", (FT, P, R1, 2 * P)),
                     ("xmid", (TILES, P, D)), ("xt", (P, KT, S))):
        t[n] = nc.dram_tensor(f"scratch_{n}", shape, F32, kind="Internal").ap()
    encoder_layer(nc, t)
    r = run_bass_kernel_spmd(nc, [{f"in_{n}": a for n, a in arrays.items()}], core_ids=[0])
    return r.results[0]["out"]
```

```python
import concourse.bass as bass
from concourse import mybir
from contextlib import ExitStack

P = 128
S = 2048
D = 1024
KT = D // P
NB = S // 512
CT = 3
FT = 2
CONV = CT * P
FOUR = FT * P
DFF = 2816
GF = 2
GROUPS = DFF // (P * GF)
TILES = S // P
R1 = 16
EPS = 1e-6
PAD = 8

F32 = mybir.dt.float32
F32R = mybir.dt.float32r
ALU = mybir.AluOpType
ACT = mybir.ActivationFunctionType


class Alloc:

    def __init__(self, nc):
        self.nc, self.stack = nc, ExitStack()

    def __enter__(self):
        self.stack.__enter__()
        return self

    def __exit__(self, *e):
        return self.stack.__exit__(*e)

    def sem(self, name):
        return self.stack.enter_context(self.nc.semaphore(name))

    def block(self):
        return self.stack.enter_context(self.nc.Block())


def mm3(nc, out, terms):
    last = len(terms) - 1
    for n, ((a_hi, a_lo), (b_hi, b_lo)) in enumerate(terms):
        nc.tensor.matmul(out, a_hi, b_hi, start=(n == 0), stop=False)
        nc.tensor.matmul(out, a_hi, b_lo, start=False, stop=False)
        ins = nc.tensor.matmul(out, a_lo, b_hi, start=False, stop=(n == last))
    return ins


def split_lo(nc, out, whole, hi):
    return nc.vector.tensor_tensor(out, whole, hi.bitcast(F32), ALU.subtract)


def place(nc, start, *tensors):
    with ExitStack() as stack:
        if start:
            stack.enter_context(nc.sbuf_tensor(f"below_{tensors[0][0]}", [P, start // 4], F32))
        return [stack.enter_context(nc.sbuf_tensor(name, shape, *(dt or [F32])))
                for name, shape, *dt in tensors]


def pair(name, shape):
    return (name + "_hi", shape, F32R), (name + "_lo", shape, F32R)


K = 1024
HALF_K = K // 2
AT_SMALL = 0
AT_R0 = 3 * HALF_K
AT_R1 = AT_R0 + 32 * K
AT_UF = AT_R1 + 32 * K
AT_REST = AT_UF + 16 * K
AT_W = AT_REST
AT_X = AT_W + 36 * K
AT_POOL = AT_X + 20 * K
AT_PR = AT_POOL + 17 * K
AT_CONV = AT_PR + 25 * HALF_K
AT_WP = AT_CONV + 59 * (K // 4)
AT_YP = AT_WP + 9 * K
AT_G3 = AT_YP + 25 * (K // 4)
AT_YS = AT_REST
AT_RAW = AT_YS + 56 * K
AT_YSRAW = AT_RAW + 12 * K
AT_XFA = AT_YSRAW + 10 * K
AT_W13 = AT_XFA + 32 * K


def stage_ab(nc, t, m, block, ident, ps, uf):
    BT = 4
    NT = 14
    LASTB = NB - 1
    TILES_Z = NT * NB
    HALO = 2 * PAD
    PW = HALO + 512 + PAD
    OW = 512 + PAD
    STEPS = 3
    F_TILES = range(2, 8)
    CH = 4
    MB = P // 4
    NCH = FT * MB // CH
    F3_TILES = {10: range(0, 4), 11: range(4, 8), 12: range(8, 12), 13: range(12, 16)}
    CUTS_F = (0, 2, 3, 4, 5, 7, 8)
    CUTS_3 = (0, 2, 4, 6, 8)

    x_v = t["x"].rearrange("o (n p) d -> (o n) p d", p=P)
    w_v = t["w_in"].rearrange("o (k p) c -> p (o k) c", p=P)
    wo_v = t["w_out"].rearrange("o (k p) d -> p (o k) d", p=P)

    wconv, invw, invcnt, edge, ss, rstd, consts, pscale = place(
        nc, AT_SMALL + 512, ("wconv", [P, CT, 3]), ("invw", [P, CT]), ("invcnt", [P, CT, 2 * PAD]),
        ("edge", [P, 2 * PAD]), ("ss", [P, 2]), ("rstd", [P, 2]), ("consts", [P, 2]),
        ("pscale", [P, CT]))
    xT = [place(nc, at, *pair(f"xT{s}", [P, KT, 512])) for s, at in enumerate((AT_R0, AT_R1))]
    w_hi, w_lo, w_raw = place(nc, AT_W, *pair("w", [P, 3, KT, P]), ("w_raw", [P, 3, KT, P]))
    x_in, xn, g_b = place(nc, AT_X, ("x_in", [P, 2, D]), ("xn", [P, 2, D]), ("g_b", [P, D]))
    pb, sums, pooled = place(nc, AT_POOL, ("pb", [P, CT, PW]), ("sums", [P, 2, PW]), ("pooled", [P, CT, OW]))
    pr_hi, pr_lo = place(nc, AT_PR, *pair("pr", [P, CT, OW]))
    X, ub, bb = place(nc, AT_CONV, ("X", [P, 514]), ("ub", [P, CT, 516]), ("bb", [P, CT, 514]))
    wp_hi, wp_lo = place(nc, AT_WP, *pair("wp", [P, CT, CT * P]))
    (yp,) = place(nc, AT_YP, ("yp", [P, CT, OW]))
    wp_raw, dft, wf = place(nc, AT_G3, ("wp_raw", [P, CT, CT * P]), ("dft", [P, 2, P]), ("wf", [P, FT, P]))
    m_hi, m_lo, us_hi, us_lo, tw_raw, tw_hi, tw_lo, ab_hi, ab_lo, g = place(
        nc, AT_R0, *pair("m", [P, FT, 3 * P]), *pair("us", [P, 2, FT, P]), ("tw_raw", [P, 2, 2, P]),
        *pair("tw", [P, 2, 2, P]), *pair("ab", [P, 2, FT, 3 * P]), ("g", [P, 2, 2, FT, P]))
    (g3,) = place(nc, AT_X, ("g3", [P, MB, FT, P]))
    g3_hi, g3_lo, t16, t16_hi, t16_lo = place(
        nc, AT_G3, *pair("g3s", [P, 2, CH, P]), ("t16", [P, 64]), *pair("t16", [P, 64]))
    wo = [place(nc, at, *pair(f"wo{e}", [P, KT, 512])) for e, at in enumerate((AT_R0, AT_R1))]

    c_ld, x_c_ld = m.sem("a_c_ld"), m.sem("a_x_c_ld")
    t16_ld = m.sem("a_t16_ld")
    x_ld = [m.sem(f"a_x_ld{i}") for i in range(2)]
    w_ld = [m.sem(f"a_w_ld{i}") for i in range(3)]
    tw_ld = [m.sem(f"a_tw_ld{i}") for i in range(2)]
    g_st = [m.sem(f"a_g_st{i}") for i in range(2)]
    g3_ld = [m.sem(f"a_g3_ld{i}") for i in range(4)]
    cy_st, py_st = m.sem("a_cy_st"), m.sem("a_py_st")
    zeroed, init = m.sem("a_zeroed"), m.sem("a_init")
    consts_set, sq_done, ms_done, rstd_done, xn_done, tr_done, xhi_done, xlo_done = (
        m.sem(f"a_{n}") for n in ("consts", "sq", "ms", "rstd", "xn", "tr", "xhi", "xlo"))
    whi_done, wlo_done = m.sem("a_whi"), m.sem("a_wlo")
    z_mm = m.sem("a_z_mm")
    act_ev, dve_ev = m.sem("a_act_ev"), m.sem("a_dve_ev")
    tap0, tap1, tap2, conv_done, carried = (m.sem(f"a_{n}") for n in ("tap0", "tap1", "tap2", "conv", "carried"))
    pstep, pool_done = m.sem("a_pstep"), m.sem("a_pool")
    wph, wpl, prh, prl, p_mm, p_ev = (m.sem(f"a_{n}") for n in ("wph", "wpl", "prh", "prl", "p_mm", "p_ev"))
    mix_mm, mhi, mlo = m.sem("f_mix_mm"), m.sem("f_mhi"), m.sem("f_mlo")
    ush, usl, twh, twl = (m.sem(f"f_{n}") for n in ("ush", "usl", "twh", "twl"))
    f1_mm, abh, abl, f2_mm, g_ev = (m.sem(f"f_{n}") for n in ("f1_mm", "abh", "abl", "f2_mm", "g_ev"))
    t16h, t16l, g3h, g3l, f3_mm, f3_ev = (m.sem(f"f_{n}") for n in ("t16h", "t16l", "g3h", "g3l", "f3_mm", "f3_ev"))

    def h_tile(G):
        return G % NT >= 5 and (G % NT - 5) % 3 == 1

    def evacuated(G):
        if h_tile(G):
            return dve_ev, sum(h_tile(x) for x in range(G + 1))
        return act_ev, sum(not h_tile(x) for x in range(G + 1))

    def w_dest(G):
        if G < TILES_Z:
            return w_hi[:, G % 3, :, :], w_lo[:, G % 3, :, :]
        e, j = divmod(G - TILES_Z, 4)
        return tuple(x[:, 2 * j:2 * j + 2, :] for x in wo[e])

    def w_src(G):
        raw = w_raw[:, G % 3, :, :]
        return raw if G < TILES_Z else raw.rearrange("p a b -> p (a b)").rearrange("p (k d) -> p k d", k=2)

    def w_free(engine, G):
        if G < TILES_Z:
            if G >= 3:
                engine.wait_ge(z_mm, G - 2)
        elif G == TILES_Z:
            engine.wait_ge(f2_mm, R1)
            engine.wait_ge(g_ev, R1)
            for s in range(2):
                engine.wait_ge(g_st[s], 16 * R1 // 2)
        elif G == TILES_Z + 4:
            engine.wait_ge(z_mm, TILES_Z)

    def next_tile(b, k):
        return BT * (b + 1) + (k - 2) // 3 if b < LASTB and k in (2, 5, 8, 11) else None

    def steps_of(b, k):
        return [STEPS * (k - F_TILES[0]) + j for j in range(STEPS)] if b == LASTB and k in F_TILES else []

    def chunks_of(b, k):
        return F3_TILES.get(k, ()) if b == LASTB else ()

    pieces = [(j, r // P, r % P, r - 96 * j, n) for j in range(4)
              for r, n in ([(0, 96)], [(96, 32), (128, 64)], [(192, 64), (256, 32)], [(288, 96)])[j]]
    NC = 5 + 2 * FT + len(pieces)

    def w_load(sp, G):
        if G >= 3:
            sp.wait_ge(wlo_done, G - 2)
        if G < TILES_Z:
            k = G % NT
            col = 3 * CONV + k * P
            if k >= 5:
                q, r = divmod(k - 5, 3)
                col = (CONV, 2 * CONV, 0)[r] + q * P
            src = w_v[:, :, col:col + P]
        else:
            e, j = divmod(G - TILES_Z, 4)
            rows = (slice(0, 2), slice(2, 6, 3), slice(6, 8), slice(3, 5))[j]
            src = wo_v[:, rows, e * 512:(e + 1) * 512]
        sp.dma_start(w_src(G), src).then_inc(w_ld[G % 3], 16)

    def w_split_hi(act, G):
        act.wait_ge(w_ld[G % 3], 16 * (G // 3 + 1))
        w_free(act, G)
        nc.scalar.activation(w_dest(G)[0], w_src(G), ACT.Copy).then_inc(whi_done, 1)

    def w_split_lo(dve, G):
        dve.wait_ge(whi_done, G + 1)
        split_lo(nc, w_dest(G)[1], w_src(G), w_dest(G)[0]).then_inc(wlo_done, 1)

    def evac(act, G, dst):
        act.wait_ge(z_mm, G + 1)
        nc.scalar.activation(dst, ps[:, 4 + G % 3, :], ACT.Copy).then_inc(act_ev, 1)


    def conv_of(G):
        b, k = divmod(G, NT)
        q = (k - 5) // 3
        return b, q, CT * b + q, 513 if b == LASTB else 512

    def conv_first(act, G):
        b, q, n, W = conv_of(G)
        act.wait_ge(dve_ev, n + 1)
        nc.scalar.activation(X[:, 0:W], ub[:, q, 0:W], ACT.Copy, scale=wconv[:, q, 0:1]).then_inc(tap0, 1)
        if b:
            act.wait_ge(carried, n - CT + 1)
        evac(act, G, bb[:, q, 1:513])

    def conv_rest(dve, G):
        b, q, n, W = conv_of(G)
        dve.wait_ge(tap0, n + 1)
        dve.wait_ge(dve_ev, n + 1)
        nc.vector.scalar_tensor_tensor(out=X[:, 0:W], in0=ub[:, q, 1:1 + W], scalar=wconv[:, q, 1:2],
                                       in1=X[:, 0:W], op0=ALU.mult, op1=ALU.add).then_inc(tap1, 1)
        dve.wait_ge(tap1, n + 1)
        nc.vector.scalar_tensor_tensor(out=X[:, 0:W], in0=ub[:, q, 2:2 + W], scalar=wconv[:, q, 2:3],
                                       in1=X[:, 0:W], op0=ALU.mult, op1=ALU.add).then_inc(tap2, 1)
        dve.wait_ge(tap2, n + 1)
        dve.wait_ge(act_ev, evacuated(G)[1])
        nc.vector.tensor_tensor(X[:, 0:W], X[:, 0:W], bb[:, q, 0:W], ALU.mult).then_inc(conv_done, 1)
        if b < LASTB:
            dve.wait_ge(conv_done, n + 1)
            nc.vector.tensor_copy(ub[:, q, 0:2], ub[:, q, 512:514])
            nc.vector.tensor_copy(bb[:, q, 0:1], bb[:, q, 512:513]).then_inc(carried, 1)

    def conv_store(sp, G):
        b, q, n, W = conv_of(G)
        sp.wait_ge(conv_done, n + 1)
        c0 = 1 if b == 0 else 0
        t0 = 512 * b - 1
        sp.dma_start(t["yd"][:, q, t0 + c0:t0 + W], X[:, c0:W]).then_inc(cy_st, 16)

    @block.sync
    def _(sp):
        def x_load(n):
            if n >= 2:
                sp.wait_ge(xn_done, n - 1)
            sp.dma_start(x_in[:, n % 2, :], x_v[n, :, :]).then_inc(x_ld[n % 2], 16)

        x_load(0)
        sp.dma_start(g_b[:, :], t["g_mix"].to_broadcast([P, D])).then_inc(x_c_ld, 16)
        sp.dma_start(ident[:, :], t["ident"]).then_inc(x_c_ld, 16)
        x_load(1)
        w_load(sp, 0)
        x_load(2)
        x_load(3)
        w_load(sp, 1)
        w_load(sp, 2)
        for dst, src in ((wconv[:, :, :], "wconv"), (invw[:, :], "invw"), (invcnt[:, :, :], "invcnt"),
                         (pscale[:, :], "pscale"), (dft[:, :, :], "dft64")):
            sp.dma_start(dst, t[src]).then_inc(c_ld, 16)
        sp.wait_ge(zeroed, 1)
        for h in range(2 * FT):
            lane = slice(64 * (h % 2), 64 * (h % 2) + 64)
            sp.dma_start(wf[lane, h // 2, lane], t["w_fourier"][0, h, :, :]).then_inc(c_ld, 16)
        for j, tile, p0, r0, n in pieces:
            sp.dma_start(wp_raw[p0:p0 + n, tile, 96 * j:96 * j + 96], t["w_pool"][0, j, r0:r0 + n, :]
                         ).then_inc(c_ld, 16)
        x_load(4)

        def tw_load(n):
            if n >= 2:
                sp.wait_ge(twl, n - 1)
            sp.dma_start(tw_raw[:, n % 2, :, :], t["tw"][:, n, :, :]).then_inc(tw_ld[n % 2], 16)

        for G in range(TILES_Z):
            b, k = divmod(G, NT)
            w_load(sp, G + 3)
            if G == TILES_Z - 1:
                w_load(sp, G + 4)
            if b < LASTB and k in (0, 3, 6, 9):
                n = BT * (b + 1) + k // 3 + 1
                if n < TILES:
                    x_load(n)
            if b == LASTB and k == 1:
                sp.wait_ge(z_mm, NT * LASTB)
                tw_load(0)
                tw_load(1)
            for s in steps_of(b, k):
                if s + 2 < R1:
                    tw_load(s + 2)
                if s >= 2:
                    n = s - 2
                    sp.wait_ge(g_ev, n + 1)
                    sp.dma_start(t["g"][:, n, :], g[:, n % 2, :, :, :].rearrange("p i c x -> p (i c x)")
                                 ).then_inc(g_st[n % 2], 16)
            if b == LASTB and k == 8:
                for s in range(2):
                    sp.wait_ge(g_st[s], 16 * R1 // 2)
                sp.wait_ge(prl, NB)
                sp.wait_ge(wpl, 1)
                sp.wait_ge(mix_mm, 1)
                sp.dma_start(t16[:, :], t["t16"]).then_inc(t16_ld, 16)
                for i in range(4):
                    for a in range(4):
                        b0 = i * MB // 4
                        k2 = slice(32 * a + b0, 32 * a + b0 + MB // 4)
                        sp.dma_start(g3[32 * a:32 * a + 32, b0:b0 + MB // 4, :, :].rearrange("p b c x -> p b (c x)"),
                                     t["g"][k2, :, :].rearrange("b n (i x) -> (n i) b x", i=2)
                                     ).then_inc(g3_ld[i], 16)
            if k == 9:
                sp.wait_ge(p_ev, CT * (b + 1) + (b == LASTB))
                c0, c1 = (PAD if b == 0 else 0), (OW if b == LASTB else 512)
                t0 = 512 * b - PAD
                sp.dma_start(t["yd"][:, CT:2 * CT, t0 + c0:t0 + c1], yp[:, :, c0:c1]).then_inc(py_st, 16)
            if k >= 5 and (k - 5) % 3 == 2:
                if G < TILES_Z - 1:
                    conv_store(sp, G)

    @block.gpsimd
    def _(pool):
        nc.gpsimd.memset(consts[:, 0:1], -0.5)
        nc.gpsimd.memset(consts[:, 1:2], EPS).then_inc(consts_set, 1)
        pool.wait_ge(consts_set, 1)
        for n in range(TILES):
            s = slice(n % 2, n % 2 + 1)
            pool.wait_ge(sq_done, n + 1)
            nc.gpsimd.tensor_tensor(ss[:, s], ss[:, s], consts[:, 1:2], ALU.add).then_inc(ms_done, 1)
            pool.wait_ge(ms_done, n + 1)
            if n >= 2:
                pool.wait_ge(xn_done, n - 1)
            nc.gpsimd.tensor_tensor(rstd[:, s], ss[:, s], consts[:, 0:1], ALU.pow).then_inc(rstd_done, 1)

    @block.scalar
    def _(act):
        def square(n):
            act.wait_ge(x_ld[n % 2], 16 * (n // 2 + 1))
            if n >= 2:
                act.wait_ge(tr_done, n - 1)
                act.wait_ge(rstd_done, n - 1)
            nc.scalar.activation(xn[:, n % 2, :], x_in[:, n % 2, :], ACT.Square, scale=D ** -0.5,
                                 accum_out=ss[:, n % 2:n % 2 + 1]).then_inc(sq_done, 1)

        def x_hi(n):
            b, j = divmod(n, BT)
            act.wait_ge(tr_done, n + 1)
            if j == 0 and b >= 2:
                act.wait_ge(z_mm, NT * (b - 1))
            for i in range(2):
                ins = nc.scalar.activation(xT[b % 2][0][:, 4 * i:4 * i + 4, j * P:(j + 1) * P],
                                           ps[:, i, :].rearrange("p (k t) -> p k t", k=4), ACT.Copy)
            ins.then_inc(xhi_done, 1)

        uf_v = uf[:, :, :].rearrange("p c (n r) -> p r c n", r=R1)

        def us(n):
            if n >= 2:
                act.wait_ge(f1_mm, n - 1)
            nc.scalar.activation(us_hi[:, n % 2, :, :], uf_v[:, n, :, :], ACT.Copy).then_inc(ush, 1)

        def step(s):
            if s < R1:
                act.wait_ge(f1_mm, s + 1)
                if s >= 2:
                    act.wait_ge(f2_mm, s - 1)
                for c in range(FT):
                    ins = nc.scalar.activation(ab_hi[:, s % 2, c, :], ps[:, 2 * (s % 2) + c, 0:3 * P],
                                               ACT.Copy)
                ins.then_inc(abh, 1)
                if s + 2 < R1:
                    us(s + 2)
                act.wait_ge(tw_ld[s % 2], 16 * (s // 2 + 1))
                nc.scalar.activation(tw_hi[:, s % 2, :, :], tw_raw[:, s % 2, :, :], ACT.Copy).then_inc(twh, 1)
            if s >= 2:
                n = s - 2
                act.wait_ge(f2_mm, n + 1)
                if n >= 2:
                    act.wait_ge(g_st[n % 2], 16 * (n // 2))
                nc.scalar.activation(g[:, n % 2, :, :, :], ps[:, 7, :].rearrange(
                    "p (c i x) -> p i c x", c=FT, i=2), ACT.Copy).then_inc(g_ev, 1)

        def f3_split(c):
            if c == 0:
                act.wait_ge(t16_ld, 16)
                nc.scalar.activation(t16_hi[:, :], t16[:, :], ACT.Copy).then_inc(t16h, 1)
            if c >= 2:
                act.wait_ge(f3_mm, c - 1)
            j, ct = divmod(c, FT)
            act.wait_ge(g3_ld[j * CH // (MB // 4)], 64)
            nc.scalar.activation(g3_hi[:, c % 2, :, :], g3[:, j * CH:(j + 1) * CH, ct, :], ACT.Copy
                                 ).then_inc(g3h, 1)

        def f3_evac(c):
            j, ct = divmod(c, FT)
            act.wait_ge(f3_mm, c + 1)
            out = uf[:, ct, :].rearrange("p (m b) -> p b m", b=MB)[:, j * CH:(j + 1) * CH, :]
            nc.scalar.activation(out, ps[:, c % 4, 0:64 * CH].rearrange("p (b m) -> p b m", b=CH), ACT.Copy
                                 ).then_inc(f3_ev, 1)

        square(0)
        square(1)
        w_split_hi(act, 0)
        act.wait_ge(x_c_ld, 32)
        for n in range(BT):
            x_hi(n)
            if n + 2 < BT:
                square(n + 2)
            if n == 0:
                w_split_hi(act, 1)
        act.wait_ge(c_ld, 16 * NC)
        nc.scalar.activation(wp_hi[:, :, :], wp_raw[:, :, :], ACT.Copy).then_inc(wph, 1)

        for G in range(TILES_Z):
            b, k = divmod(G, NT)
            w_split_hi(act, G + 2)
            if k == NT - 1 and b == LASTB:
                w_split_hi(act, TILES_Z + 2)
                w_split_hi(act, TILES_Z + 3)
            if (n := next_tile(b, k)) is not None:
                x_hi(n)
            if b == LASTB and k == 0:
                act.wait_ge(mix_mm, 1)
                for c in range(FT):
                    nc.scalar.activation(m_hi[:, c, P:3 * P], ps[:, c, 0:2 * P], ACT.Copy)
                    ins = nc.scalar.activation(m_hi[:, c, 0:P], ps[:, c, P:2 * P], ACT.Copy, scale=-1.0)
                ins.then_inc(mhi, 1)
            for s in steps_of(b, k):
                step(s)
            for c in chunks_of(b, k):
                if c + 2 < NCH:
                    f3_split(c + 2)
                f3_evac(c)
            if k < 2:
                evac(act, G, uf[:, k, b * 512:(b + 1) * 512])
                if b == LASTB and k == 1:
                    act.wait_ge(act_ev, evacuated(G)[1])
                    us(0)
                    us(1)
            elif k < 5:
                i = k - 2
                act.wait_ge(init, 1)
                if b:
                    act.wait_ge(pool_done, CT * (b - 1) + i + 1)
                evac(act, G, pb[:, i, HALO:HALO + 512])
            else:
                q, r = divmod(k - 5, 3)
                n = CT * b + q
                if r == 0:
                    if n:
                        act.wait_ge(cy_st, 16 * n)
                    evac(act, G, X[:, 0:512])
                elif r == 2:
                    if G < TILES_Z - 1:
                        conv_first(act, G)
            if k == 5 + (b == LASTB):
                act.wait_ge(pool_done, CT * (b + 1))
                if b:
                    act.wait_ge(p_mm, CT * b)
                w = OW if b == LASTB else 512
                nc.scalar.activation(pr_hi[:, :, 0:w], pooled[:, :, 0:w], ACT.Copy).then_inc(prh, 1)
            if k in (8, 9):
                if k == 8 and b:
                    act.wait_ge(py_st, 16 * b)
                for o in ((0, 1), (2,))[k - 8]:
                    act.wait_ge(p_mm, CT * b + o + 1)
                    nc.scalar.activation(yp[:, o, 0:512], ps[:, 2 + o % 2, :], ACT.Copy,
                                         scale=pscale[:, o:o + 1]).then_inc(p_ev, 1)
                if b == LASTB and k == 9:
                    act.wait_ge(p_mm, CT * NB + 1)
                    for o in range(CT):
                        ins = nc.scalar.activation(yp[:, o, 512:OW], ps[:, 7, o * PAD:(o + 1) * PAD], ACT.Copy,
                                                   scale=pscale[:, o:o + 1])
                    ins.then_inc(p_ev, 1)
            if b < LASTB and k in (0, 2, 5, 8):
                square(BT * (b + 1) + (k + 1) // 3)
            if b == LASTB and k == 9:
                f3_split(0)
                f3_split(1)

    @block.vector
    def _(dve):
        uf_v = uf[:, :, :].rearrange("p c (n r) -> p r c n", r=R1)

        def norm(n):
            dve.wait_ge(rstd_done, n + 1)
            nc.vector.scalar_tensor_tensor(out=xn[:, n % 2, :], in0=x_in[:, n % 2, :],
                                           scalar=rstd[:, n % 2:n % 2 + 1], in1=g_b[:, :], op0=ALU.mult,
                                           op1=ALU.mult).then_inc(xn_done, 1)

        def x_lo(n):
            b, j = divmod(n, BT)
            dve.wait_ge(xhi_done, n + 1)
            for i in range(2):
                sel = (slice(None), slice(4 * i, 4 * i + 4), slice(j * P, (j + 1) * P))
                ins = split_lo(nc, xT[b % 2][1][sel], ps[:, i, :].rearrange("p (k t) -> p k t", k=4),
                               xT[b % 2][0][sel])
            ins.then_inc(xlo_done, 1)

        steps = [0]

        def chain(ins):
            steps[0] += 1
            ins.then_inc(pstep, 1)
            dve.wait_ge(pstep, steps[0])

        def window_sums(i, b):
            E = PW if b == LASTB else PW - PAD
            U, A, B = pb[:, i, :], sums[:, 0, :], sums[:, 1, :]

            def double(dst, src, by, margin, parts):
                lo, hi = margin, E - margin
                for p0, p1 in parts:
                    chain(nc.vector.tensor_tensor(dst[p0:p1, lo:hi], src[p0:p1, lo - by:hi - by],
                                                  src[p0:p1, lo + by:hi + by], ALU.add))

            whole = [(0, P)]
            chain(nc.vector.tensor_tensor(A[:, 1:E], U[:, 0:E - 1], U[:, 1:E], ALU.add))
            if i == 0:
                double(B, A, 1, 2, [(96, P)])
                return [(0, 96, A), (96, P, B)]
            double(B, A, 1, 2, whole)
            if i == 1:
                double(A, B, 2, 4, [(64, P)])
                return [(0, 64, B), (64, P, A)]
            double(A, B, 2, 4, whole)
            double(B, A, 4, 8, [(32, 64), (64, P)])
            return [(0, 32, A), (32, 64, B), (64, P, B)]

        def window_means(i, b, parts):
            E = PW if b == LASTB else PW - PAD
            U = pb[:, i, :]
            for p0, p1, w in parts:
                chain(nc.vector.scalar_tensor_tensor(
                    out=pooled[p0:p1, i, 0:E - 2 * PAD], in0=w[p0:p1, PAD:E - PAD],
                    scalar=invw[p0:p1, i:i + 1], in1=U[p0:p1, PAD:E - PAD], op0=ALU.mult,
                    op1=ALU.subtract))
                if b in (0, LASTB):
                    e, c0 = (0, HALO) if b == 0 else (1, HALO + 512 - PAD)
                    ed = edge[p0:p1, e * PAD:(e + 1) * PAD]
                    chain(nc.vector.tensor_tensor(ed, w[p0:p1, c0:c0 + PAD],
                                                  invcnt[p0:p1, i, e * PAD:(e + 1) * PAD], ALU.mult))
                    chain(nc.vector.tensor_tensor(pooled[p0:p1, i, c0 - PAD:c0], ed, U[p0:p1, c0:c0 + PAD],
                                                  ALU.subtract))
            nc.vector.tensor_copy(U[:, 0:HALO], U[:, 512:512 + HALO]).then_inc(pool_done, 1)

        def step(s):
            if s < R1:
                dve.wait_ge(abh, s + 1)
                for c in range(FT):
                    ins = split_lo(nc, ab_lo[:, s % 2, c, :], ps[:, 2 * (s % 2) + c, 0:3 * P],
                                   ab_hi[:, s % 2, c, :])
                ins.then_inc(abl, 1)
                if s + 2 < R1:
                    us(s + 2)
                dve.wait_ge(twh, s + 1)
                split_lo(nc, tw_lo[:, s % 2, :, :], tw_raw[:, s % 2, :, :], tw_hi[:, s % 2, :, :]
                         ).then_inc(twl, 1)

        def us(n):
            dve.wait_ge(ush, n + 1)
            split_lo(nc, us_lo[:, n % 2, :, :], uf_v[:, n, :, :], us_hi[:, n % 2, :, :]).then_inc(usl, 1)

        def f3_split(c):
            j, ct = divmod(c, FT)
            if c == 0:
                dve.wait_ge(t16h, 1)
                split_lo(nc, t16_lo[:, :], t16[:, :], t16_hi[:, :]).then_inc(t16l, 1)
            dve.wait_ge(g3h, c + 1)
            split_lo(nc, g3_lo[:, c % 2, :, :], g3[:, j * CH:(j + 1) * CH, ct, :], g3_hi[:, c % 2, :, :]
                     ).then_inc(g3l, 1)

        nc.vector.memset(wf[:, :, :], 0.0)
        nc.vector.memset(wp_raw[:, :, :], 0.0).then_inc(zeroed, 1)
        nc.vector.memset(pb[:, :, :], 0.0)
        nc.vector.memset(ub[:, :, :], 0.0)
        nc.vector.memset(bb[:, :, :], 0.0).then_inc(init, 1)
        dve.wait_ge(x_c_ld, 32)
        norm(0)
        norm(1)
        for n in range(BT):
            x_lo(n)
            if n + 2 < BT:
                norm(n + 2)
            if n < 2:
                w_split_lo(dve, n)
        dve.wait_ge(wph, 1)
        split_lo(nc, wp_lo[:, :, :], wp_raw[:, :, :], wp_hi[:, :, :]).then_inc(wpl, 1)
        dve.wait_ge(init, 1)

        for G in range(TILES_Z):
            b, k = divmod(G, NT)
            w_split_lo(dve, G + 2)
            if k == NT - 1 and b == LASTB:
                w_split_lo(dve, TILES_Z + 2)
                w_split_lo(dve, TILES_Z + 3)
            if b < LASTB and k in (1, 3, 6, 9):
                norm(BT * (b + 1) + k // 3)
            if (n := next_tile(b, k)) is not None:
                x_lo(n)
            if b == LASTB and k == 0:
                dve.wait_ge(mhi, 1)
                for c in range(FT):
                    split_lo(nc, m_lo[:, c, P:3 * P], ps[:, c, 0:2 * P], m_hi[:, c, P:3 * P])
                    ins = nc.vector.scalar_tensor_tensor(out=m_lo[:, c, 0:P], in0=ps[:, c, P:2 * P],
                                                         scalar=-1.0, in1=m_hi[:, c, 0:P].bitcast(F32),
                                                         op0=ALU.mult, op1=ALU.subtract)
                ins.then_inc(mlo, 1)
            for j, s in enumerate(steps_of(b, k)):
                step(s)
                if k in (3, 4, 5) and j == 0:
                    parts = window_sums(k - 3, b)
                elif k in (3, 4, 5) and j == 1:
                    window_means(k - 3, b, parts)
            for c in chunks_of(b, k):
                if c + 2 < NCH:
                    f3_split(c + 2)
            if b == LASTB and k == 1:
                us(0)
                us(1)
            if 2 <= k < 5:
                if k == 2 and b:
                    dve.wait_ge(prl, b)
                dve.wait_ge(act_ev, evacuated(G)[1])
                if b < LASTB:
                    window_means(k - 2, b, window_sums(k - 2, b))
            elif k >= 5:
                q, r = divmod(k - 5, 3)
                n = CT * b + q
                if r == 1:
                    dve.wait_ge(act_ev, evacuated(G - 1)[1])
                    dve.wait_ge(z_mm, G + 1)
                    if b:
                        dve.wait_ge(carried, n - CT + 1)
                    nc.vector.tensor_tensor(ub[:, q, 2:514], ps[:, 4 + G % 3, :], X[:, 0:512], ALU.mult
                                            ).then_inc(dve_ev, 1)
                elif r == 2:
                    if G < TILES_Z - 1:
                        conv_rest(dve, G)
            if k == 6 + (b == LASTB):
                dve.wait_ge(prh, b + 1)
                w = OW if b == LASTB else 512
                split_lo(nc, pr_lo[:, :, 0:w], pooled[:, :, 0:w], pr_hi[:, :, 0:w]).then_inc(prl, 1)
            if b == LASTB and k == 9:
                f3_split(0)
                f3_split(1)

    @block.tensor
    def _(pe):
        def transposes(n):
            pe.wait_ge(xn_done, n + 1)
            if n:
                pe.wait_ge(xlo_done, n)
            for k in range(KT):
                ins = nc.tensor.transpose(ps[:, k // 4, (k % 4) * P:(k % 4 + 1) * P],
                                          xn[:, n % 2, k * P:(k + 1) * P], ident[:, :])
            ins.then_inc(tr_done, 1)

        def product(G, c0, c1):
            if c0 == 0:
                pe.wait_ge(wlo_done, G + 1)
                if G >= 3:
                    pe.wait_ge(*evacuated(G - 3))
            xb = xT[G // NT % 2]
            for c in range(c0, c1):
                a, x = (w_hi[:, G % 3, c, :], w_lo[:, G % 3, c, :]), (xb[0][:, c, :], xb[1][:, c, :])
                out = ps[:, 4 + G % 3, :]
                nc.tensor.matmul(out, a[0], x[0], start=(c == 0), stop=False)
                nc.tensor.matmul(out, a[0], x[1], start=False, stop=False)
                ins = nc.tensor.matmul(out, a[1], x[0], start=False, stop=(c == KT - 1))
            if c1 == KT:
                ins.then_inc(z_mm, 1)

        def f1(n):
            pe.wait_ge(usl, n + 1)
            if n == 0:
                pe.wait_ge(mlo, 1)
                pe.wait_ge(p_ev, CT * LASTB)
            if n >= 2:
                pe.wait_ge(abl, n - 1)
            for c in range(FT):
                ins = mm3(nc, ps[:, 2 * (n % 2) + c, 0:3 * P],
                          [((us_hi[:, n % 2, c, :], us_lo[:, n % 2, c, :]), (m_hi[:, c, :], m_lo[:, c, :]))])
            ins.then_inc(f1_mm, 1)

        def f2(n):
            pe.wait_ge(abl, n + 1)
            pe.wait_ge(twl, n + 1)
            if n:
                pe.wait_ge(g_ev, n)
            s = n % 2
            terms = [((tw_hi[:, s, f, :], tw_lo[:, s, f, :]),
                      (ab_hi[:, s, :, P - f * P:3 * P - f * P], ab_lo[:, s, :, P - f * P:3 * P - f * P]))
                     for f in range(2)]
            mm3(nc, ps[:, 7, :].rearrange("p (c x) -> p c x", c=FT), terms).then_inc(f2_mm, 1)

        def f3(c):
            pe.wait_ge(g3l, c + 1)
            if c >= 4:
                pe.wait_ge(f3_ev, c - 3)
            for b in range(CH):
                ins = mm3(nc, ps[:, c % 4, b * 64:(b + 1) * 64],
                          [((g3_hi[:, c % 2, b, :], g3_lo[:, c % 2, b, :]), (t16_hi[:, :], t16_lo[:, :]))])
            ins.then_inc(f3_mm, 1)

        def pool_mix(b, o, out, c0, c1):
            tiles = ((0, 1), (0, 1, 2), (1, 2))[o]
            return mm3(nc, out, [((wp_hi[:, i, o * P:(o + 1) * P], wp_lo[:, i, o * P:(o + 1) * P]),
                                  (pr_hi[:, i, c0:c1], pr_lo[:, i, c0:c1])) for i in tiles])

        pe.wait_ge(x_c_ld, 32)
        for n in range(BT):
            transposes(n)
        for G in range(TILES_Z):
            b, k = divmod(G, NT)
            if (n := next_tile(b, k)) is not None:
                transposes(n)
            if k == 0:
                pe.wait_ge(xlo_done, BT * (b + 1))
            if b == LASTB and k == 0:
                pe.wait_ge(c_ld, 16 * NC)
                for c in range(FT):
                    for f in range(2):
                        ins = nc.tensor.matmul(ps[:, c, f * P:(f + 1) * P], dft[:, f, :], wf[:, c, :],
                                               start=True, stop=True)
                ins.then_inc(mix_mm, 1)
            if steps_of(b, k):
                for j, s in enumerate(steps_of(b, k)):
                    product(G, CUTS_F[2 * j], CUTS_F[2 * j + 1])
                    if s < R1:
                        f1(s)
                    if s >= 2:
                        f2(s - 2)
                    product(G, CUTS_F[2 * j + 1], CUTS_F[2 * j + 2])
            elif chunks_of(b, k):
                for j, c in enumerate(chunks_of(b, k)):
                    product(G, CUTS_3[j], CUTS_3[j + 1])
                    if c == 0:
                        pe.wait_ge(t16l, 1)
                        pe.wait_ge(p_ev, CT * NB + 1)
                    f3(c)
            else:
                product(G, 0, KT)
            if k in (8, 9):
                pe.wait_ge(prl, b + 1)
                pe.wait_ge(wpl, 1)
                for o in ((0, 1), (2,))[k - 8]:
                    if CT * b + o >= 2:
                        pe.wait_ge(p_ev, CT * b + o - 1 if o == 2 else CT * b)
                    if b == LASTB:
                        pe.wait_ge(abl, R1)
                    pool_mix(b, o, ps[:, 2 + o % 2, :], 0, 512).then_inc(p_mm, 1)
                if b == LASTB and k == 9:
                    pe.wait_ge(g_ev, R1)
                    for o in range(CT):
                        ins = pool_mix(b, o, ps[:, 7, o * PAD:(o + 1) * PAD], 512, OW)
                    ins.then_inc(p_mm, 1)

    return dict(wo=wo, wlo=wlo_done, z_mm=z_mm, p_mm=p_mm, g3l=g3l, f3_mm=f3_mm, f3_ev=f3_ev, cy_st=cy_st,
                py_st=py_st, act_ev=act_ev, dve_ev=dve_ev, n_wlo=(TILES_Z + 4, TILES_Z + 8), n_z=TILES_Z,
                n_p=CT * NB + 1, n_f3=NCH, n_act_ev=sum(not h_tile(x) for x in range(TILES_Z)),
                n_dve_ev=sum(h_tile(x) for x in range(TILES_Z)), last=TILES_Z - 1,
                chunks=range(TILES_Z + 4, TILES_Z + 8), w_load=w_load, w_split_hi=w_split_hi,
                w_split_lo=w_split_lo, conv_first=conv_first, conv_rest=conv_rest, conv_store=conv_store)


def stage_cd(nc, t, m, block, ident, ps, uf, ab):
    x_v = t["x"].rearrange("o (n p) d -> (o n) p d", p=P)
    xm_v = t["xmid"]
    w13_v = [t[w].rearrange("o (k p) f -> p (o k) f", p=P) for w in ("w1", "w3")]
    w2_v = t["w2"].rearrange("o (j p) d -> p (o j) d", p=P)
    HT = TILES // 2
    FW = GF * P
    XC = KT // 2
    UB = GF
    DB = 8
    LAST = 2 * GROUPS

    consts, ss, rstd = place(nc, AT_SMALL + 1024, ("cconsts", [P, 2]), ("css", [P, 2]), ("crstd", [P, 2]))
    (raw,) = place(nc, AT_RAW, ("raw", [P, 2, D]))
    (w13_raw,) = place(nc, AT_W13, ("w13_raw", [P, 2, KT, FW]))
    wo = ab["wo"]
    ys_hi, ys_lo, x_in, xm, xn, xt, g_b = place(
        nc, AT_YS, *pair("ys", [P, 2, KT, P]), ("cx_in", [P, 2, D]), ("xm", [P, 2, D]), ("cxn", [P, 2, D]),
        ("xt", [P, 2, KT, P]), ("cg_b", [P, D]))
    (ysraw,) = place(nc, AT_YSRAW, ("ysraw", [P, 2, 2 * CT, P]))
    xf = [place(nc, at, *pair(f"xf{b}", [P, KT, 512])) for b, at in enumerate((AT_XFA, AT_R1))]
    w13_hi, w13_lo = place(nc, AT_R0, *pair("w13", [P, GF, 2, KT, P]))
    w2_raw, w2_hi, w2_lo, h_hi, h_lo, acc = place(
        nc, AT_UF, ("w2_raw", [P, GF, D]), *pair("w2", [P, GF, D]), *pair("h", [P, 2, GF, 512]),
        ("acc", [P, HT, D]))
    sil, hf, gf_b, junk = place(
        nc, AT_RAW + 8 * K, ("sil", [P, GF, 512]), ("hf", [P, GF, 512]), ("gf_b", [P, D]),
        ("junk", [P, D], mybir.dt.bfloat16))

    g_ld = m.sem("c_g_ld")
    yr_ld = [m.sem(f"c_yr_ld{i}") for i in range(2)]
    x_ld = [m.sem(f"c_x_ld{i}") for i in range(2)]
    ys_h = m.sem("c_ys_h")
    ys_l = m.sem("c_ys_l")
    yf_h = m.sem("c_yf_h")
    yf_l = m.sem("c_yf_l")
    o_mm = m.sem("c_o_mm")
    xm_done = m.sem("c_xm_done")
    consts_set = m.sem("c_consts_set")
    sq_done = m.sem("c_sq_done")
    ms_done = m.sem("c_ms_done")
    rstd_done = m.sem("c_rstd_done")
    xn_done = m.sem("c_xn_done")
    tr_done = m.sem("c_tr_done")
    xt_done = m.sem("c_xt_done")
    xm_st = [m.sem(f"c_xm_st{i}") for i in range(2)]
    xt_st = [m.sem(f"c_xt_st{i}") for i in range(2)]

    xf_ld = [m.sem(f"d_xf_ld{i}") for i in range(2)]
    xfh = m.sem("d_xfh")
    xfl = m.sem("d_xfl")
    w13_ld = [m.sem(f"d_w{i}_ld") for i in (1, 3)]
    w13h = m.sem("d_w13h")
    w13l = m.sem("d_w13l")
    w2_ld = m.sem("d_w2_ld")
    w2h = m.sem("d_w2h")
    w2l = m.sem("d_w2l")
    up_mm = m.sem("d_up_mm")
    sil_done = m.sem("d_sil_done")
    hf_done = m.sem("d_hf_done")
    hh = m.sem("d_hh")
    hl = m.sem("d_hl")
    dn_mm = m.sem("d_dn_mm")
    acc_ld = [[m.sem(f"d_acc_ld{p}{b}") for b in range(2)] for p in range(2)]
    acc_done = m.sem("d_acc_done")
    gf_ld = m.sem("d_gf_ld")
    fsq = m.sem("d_fsq")
    fms = m.sem("d_fms")
    frs = m.sem("d_frs")
    o_done = m.sem("d_o_done")
    o_st = [[m.sem(f"d_o_st{p}{b}") for b in range(2)] for p in range(2)]

    def later(n):
        return not (isinstance(n, int) and n < 2)

    def rest(g):
        return not isinstance(g, int) or g > 0

    @block.sync
    def _(sp):
        def yr_load(n, s):
            if later(n):
                sp.wait_ge(ys_l, n - 1)
            sp.dma_start(ysraw[:, s, :, :], t["yd"][:, :, bass.ds(n * P, P)]).then_inc(yr_ld[s], 16)

        def x_load(n, s):
            if later(n):
                sp.wait_ge(xm_done, 2 * n - 2)
            sp.dma_start(x_in[:, s, :], x_v[bass.ds(n, 1), :, :].rearrange("o p d -> p (o d)")
                         ).then_inc(x_ld[s], 16)

        def store(n, s):
            sp.wait_ge(xm_done, 2 * n + 2)
            sp.dma_start(xm_v[bass.ds(n, 1), :, :].rearrange("o p d -> p (o d)"), xm[:, s, :]
                         ).then_inc(xm_st[s], 16)
            sp.wait_ge(xt_done, n + 1)
            sp.dma_start(t["xt"][:, :, bass.ds(n * P, P)], xt[:, s, :, :]).then_inc(xt_st[s], 16)

        def load13(i):
            for w in range(2):
                sp.dma_start(w13_raw[:, w, :, :], w13_v[w][:, :, bass.ds(i * FW, FW)]
                             ).then_inc(w13_ld[w], 16)

        def load2(i):
            sp.dma_start(w2_raw[:, :, :], w2_v[:, bass.ds(i * GF, GF), :]).then_inc(w2_ld, 16)

        def load_xf(part, b, k):
            c = (2 * part + b) * XC + k
            if c >= 2:
                sp.wait_ge(xfl, c - 1)
            sp.dma_start(raw[:, c % 2, :].rearrange("p (k t) -> p k t", k=2),
                         t["xt"][:, 2 * k:2 * k + 2, (2 * part + b) * 512:(2 * part + b + 1) * 512]
                         ).then_inc(xf_ld[c % 2], 16)

        def load_acc(part, b):
            n0 = part * HT + 4 * b
            sp.dma_start(acc[:, 4 * b:4 * b + 4, :], xm_v[n0:n0 + 4, :, :].rearrange("n p d -> p n d")
                         ).then_inc(acc_ld[part][b], 16)

        def store_out(part, b):
            for n in range(part * HT + 4 * b, part * HT + 4 * b + 4):
                sp.wait_ge(o_done, n + 1)
                sp.dma_start(t["out"][0, n * P:(n + 1) * P, :], acc[:, n % HT, :]).then_inc(o_st[part][b], 16)

        sp.wait_ge(ab["cy_st"], 16 * CT)
        sp.wait_ge(ab["py_st"], 16)
        sp.wait_ge(ab["p_mm"], ab["n_p"])
        yr_load(0, 0)
        yr_load(1, 1)
        ab["w_load"](sp, ab["chunks"][0])
        ab["w_load"](sp, ab["chunks"][1])
        sp.wait_ge(ab["z_mm"], ab["n_z"])
        x_load(0, 0)
        ab["w_load"](sp, ab["chunks"][2])
        ab["w_load"](sp, ab["chunks"][3])
        x_load(1, 1)
        sp.wait_ge(ab["g3l"], ab["n_f3"])
        sp.dma_start(g_b[:, :], t["g_ffn"].to_broadcast([P, D])).then_inc(g_ld, 16)
        ab["conv_store"](sp, ab["last"])
        yr_load(2, 0)
        sp.wait_ge(ab["f3_mm"], ab["n_f3"])
        sp.wait_ge(ab["cy_st"], 16 * CT * NB)
        sp.wait_ge(ab["py_st"], 16 * NB)

        def tile(n, s, more=True):
            if more:
                yr_load(n + 3, (s + 1) % 2)
            store(n, s)
            x_load(n + 2, s)

        tile(0, 0)
        tile(1, 1)
        load13(0)
        with sp.Fori(1, HT // 2) as i:
            for s in range(2):
                tile(2 * i + s, s)
        for n in range(HT, TILES - 2):
            if n == HT:
                for s in range(2):
                    sp.wait_ge(xt_st[s], 16 * (HT // 2))
                load_xf(0, 0, 0)
                load_xf(0, 0, 1)
            elif n < HT + XC - 1:
                load_xf(0, 0, n - HT + 1)
            elif n >= TILES - 4:
                load_xf(0, 1, n - TILES + 4)
            tile(n, n % 2, n + 3 < TILES)
        for s in range(2):
            store(TILES - 2 + s, s)
            load_xf(0, 1, 2 + s)
        sp.wait_ge(tr_done, TILES)
        for s in range(2):
            sp.wait_ge(xm_st[s], 16 * HT)
            sp.wait_ge(xt_st[s], 16 * HT)
        load2(0)
        for b in range(2):
            load_acc(0, b)
        sp.dma_start(gf_b[:, :], t["g_final"].to_broadcast([P, D])).then_inc(gf_ld, 16)

        def loads(g, i):
            sp.wait_ge(w13l, 2 * GF * g)
            load13(i)
            sp.wait_ge(w2l, g)
            load2(i)

        with sp.Fori(1, GROUPS) as i:
            loads(i, i)
        sp.wait_ge(w13l, 2 * GF * GROUPS)
        load13(0)
        for k in range(XC):
            load_xf(1, 0, k)
        sp.wait_ge(w2l, GROUPS)
        load2(0)
        for k in range(XC):
            load_xf(1, 1, k)
        sp.wait_ge(w13l, 2 * GF * (GROUPS + 1))
        load13(1)
        store_out(0, 0)
        sp.wait_ge(o_st[0][0], 16 * 4)
        load_acc(1, 0)
        store_out(0, 1)
        sp.wait_ge(w2l, GROUPS + 1)
        load2(1)
        sp.wait_ge(o_st[0][1], 16 * 4)
        load_acc(1, 1)
        with sp.Fori(2, GROUPS) as i:
            loads(GROUPS + i, i)
        for b in range(2):
            store_out(1, b)
        for b in range(2):
            sp.wait_ge(o_st[1][b], 16 * 4)

    @block.gpsimd
    def _(pool):
        nc.gpsimd.memset(consts[:, 0:1], -0.5)
        nc.gpsimd.memset(consts[:, 1:2], EPS).then_inc(consts_set, 1)
        pool.wait_ge(consts_set, 1)

        def rms(n, s, squares, mean, root):
            pool.wait_ge(squares, n + 1)
            nc.gpsimd.tensor_tensor(ss[:, s:s + 1], ss[:, s:s + 1], consts[:, 1:2], ALU.add
                                    ).then_inc(mean, 1)
            pool.wait_ge(mean, n + 1)
            nc.gpsimd.tensor_tensor(rstd[:, s:s + 1], ss[:, s:s + 1], consts[:, 0:1], ALU.pow
                                    ).then_inc(root, 1)

        with pool.Fori(0, TILES // 2) as i:
            for s in range(2):
                rms(2 * i + s, s, sq_done, ms_done, rstd_done)
        for s in range(2):
            rms(s, s, fsq, fms, frs)
        with pool.Fori(1, TILES // 2) as i:
            for s in range(2):
                pool.wait_ge(o_done, 2 * i + s - 1)
                rms(2 * i + s, s, fsq, fms, frs)

    @block.scalar
    def _(act):
        act.wait_ge(ab["z_mm"], ab["n_z"])

        def slot_free(engine, n):
            if later(n):
                engine.wait_ge(o_mm, n + 1 if isinstance(n, int) and n < 4 else 2 * n - 2)

        def ys(n, s, i):
            act.wait_ge(yr_ld[s], 16 * (i + 1))
            slot_free(act, n)
            nc.scalar.activation(ys_hi[:, s, 0:2 * CT, :], ysraw[:, s, :, :], ACT.Copy).then_inc(ys_h, 1)
            if isinstance(n, int) and n == 0:
                act.wait_ge(ab["f3_ev"], ab["n_f3"])
            nc.scalar.activation(ys_hi[:, s, 2 * CT:KT, :], uf[:, :, bass.ds(n * P, P)], ACT.Copy
                                 ).then_inc(yf_h, 1)

        def square(n, s):
            act.wait_ge(xm_done, 2 * n + 2)
            if later(n):
                act.wait_ge(tr_done, n - 1)
            nc.scalar.activation(xn[:, s, :], xm[:, s, :], ACT.Square, scale=D ** -0.5,
                                 accum_out=ss[:, s:s + 1]).then_inc(sq_done, 1)

        def evac(n, s, i=0):
            act.wait_ge(tr_done, n + 1)
            if later(n):
                act.wait_ge(xt_st[s], 16 * i)
            for b in range(2):
                ins = nc.scalar.activation(xt[:, s, 4 * b:4 * b + 4, :].rearrange("p k t -> p (k t)"),
                                           ps[:, 4 + 2 * s + b, :], ACT.Copy)
            ins.then_inc(xt_done, 1)

        def xf_split(part, b, k):
            c = (2 * part + b) * XC + k
            act.wait_ge(xf_ld[c % 2], 16 * (c // 2 + 1))
            if part and k == 0:
                act.wait_ge(up_mm, 2 * UB * (GROUPS - 1) + UB * (b + 1))
            nc.scalar.activation(xf[b][0][:, 2 * k:2 * k + 2, :],
                                 raw[:, c % 2, :].rearrange("p (k t) -> p k t", k=2), ACT.Copy
                                 ).then_inc(xfh, 1)

        def w13_split(g, f):
            for w in range(2):
                act.wait_ge(w13_ld[w], 16 * g + 16)
            if rest(g):
                act.wait_ge(up_mm, 2 * UB * g - UB + f + 1)
            for w in range(2):
                nc.scalar.activation(w13_hi[:, f, w, :, :], w13_raw[:, w, :, f * P:(f + 1) * P],
                                     ACT.Copy).then_inc(w13h, 1)

        def w2_split(g):
            act.wait_ge(w2_ld, 16 * g + 16)
            if rest(g):
                act.wait_ge(dn_mm, 2 * DB * g)
            nc.scalar.activation(w2_hi[:, :, :], w2_raw[:, :, :], ACT.Copy).then_inc(w2h, 1)

        def activate(g, b, f):
            n = 2 * UB * g + UB * b + f
            act.wait_ge(up_mm, n + 1)
            if not isinstance(g, int) or n >= GF:
                act.wait_ge(hf_done, n - 1)
            nc.scalar.activation(sil[:, f, :], ps[:, 2 * f, :], ACT.Silu).then_inc(sil_done, 1)
            act.wait_ge(hf_done, n + 1)
            nc.scalar.activation(h_hi[:, b, f, :], hf[:, f, :], ACT.Copy).then_inc(hh, 1)

        def final_square(part, b):
            for j in range(4):
                n = part * HT + 4 * b + j
                act.wait_ge(acc_done, 2 * DB * (GROUPS * (part + 1) - 1) + DB * b + 2 * j + 2)
                if n >= 1:
                    act.wait_ge(fsq, n)
                if n >= 2:
                    act.wait_ge(frs, n - 1)
                nc.scalar.activation(junk[:, :], acc[:, 4 * b + j, :], ACT.Square, scale=D ** -0.5,
                                     accum_out=ss[:, n % 2:n % 2 + 1]).then_inc(fsq, 1)

        ys(0, 0, 0)
        for c in ab["chunks"]:
            ab["w_split_hi"](act, c)
        ys(1, 1, 0)
        ab["conv_first"](act, ab["last"])
        for s in range(2):
            ys(2 + s, s, 1)
            square(s, s)
            evac(s, s)
        with act.Fori(1, HT // 2) as i:
            for s in range(2):
                ys(2 * i + 2 + s, s, i + 1)
                square(2 * i + s, s)
                evac(2 * i + s, s, i)
        for n in range(HT, TILES - 2):
            ys(n + 2, n % 2, n // 2 + 1)
            square(n, n % 2)
            evac(n, n % 2, n // 2)
            if HT < n <= HT + XC:
                xf_split(0, 0, n - HT - 1)
        square(TILES - 2, 0)
        act.wait_ge(o_mm, 2 * TILES - 1)
        w13_split(0, 0)
        evac(TILES - 2, 0, HT - 1)
        square(TILES - 1, 1)
        w13_split(0, 1)
        evac(TILES - 1, 1, HT - 1)
        act.wait_ge(o_mm, 2 * TILES)
        for k in range(XC):
            if k == 2:
                activate(0, 0, 0)
            xf_split(0, 1, k)
        w2_split(0)
        activate(0, 0, 1)

        def group(g, more):
            for f in range(GF):
                activate(g, 1, f)
                if more:
                    w13_split(g + 1, f)
            if more:
                for f in range(GF):
                    activate(g + 1, 0, f)
                w2_split(g + 1)

        with act.Fori(0, GROUPS - 1) as i:
            group(i, True)
        g = GROUPS - 1
        for k in range(XC):
            xf_split(1, 0, k)
        for f in range(GF):
            activate(g, 1, f)
            w13_split(g + 1, f)
        for k in range(XC):
            xf_split(1, 1, k)
        final_square(0, 0)
        for f in range(GF):
            activate(g + 1, 0, f)
        w2_split(g + 1)
        final_square(0, 1)
        with act.Fori(GROUPS, LAST - 1) as i:
            group(i, True)
        group(LAST - 1, False)
        final_square(1, 0)
        final_square(1, 1)

    @block.vector
    def _(dve):
        def ys(n, s):
            dve.wait_ge(ys_h, n + 1)
            split_lo(nc, ys_lo[:, s, 0:2 * CT, :], ysraw[:, s, :, :], ys_hi[:, s, 0:2 * CT, :]
                     ).then_inc(ys_l, 1)
            dve.wait_ge(yf_h, n + 1)
            split_lo(nc, ys_lo[:, s, 2 * CT:KT, :], uf[:, :, bass.ds(n * P, P)], ys_hi[:, s, 2 * CT:KT, :]
                     ).then_inc(yf_l, 1)

        def residual(n, s, i=0, halves=range(2)):
            dve.wait_ge(x_ld[s], 16 * (i + 1))
            if later(n):
                dve.wait_ge(xm_st[s], 16 * i)
                dve.wait_ge(xn_done, n - 1)
            for b in halves:
                dve.wait_ge(o_mm, n + 2 * b + 1 if isinstance(n, int) and n < 2 else 2 * n + b + 1)
                nc.vector.tensor_tensor(xm[:, s, b * 512:(b + 1) * 512], ps[:, 2 * s + b, :],
                                        x_in[:, s, b * 512:(b + 1) * 512], ALU.add
                                        ).then_inc(xm_done, 1)

        def norm(n, s):
            dve.wait_ge(rstd_done, n + 1)
            nc.vector.scalar_tensor_tensor(out=xn[:, s, :], in0=xm[:, s, :],
                                           scalar=rstd[:, s:s + 1], in1=g_b[:, :], op0=ALU.mult,
                                           op1=ALU.mult).then_inc(xn_done, 1)

        def xf_split(part, b, k):
            c = (2 * part + b) * XC + k
            dve.wait_ge(xfh, c + 1)
            split_lo(nc, xf[b][1][:, 2 * k:2 * k + 2, :], raw[:, c % 2, :].rearrange("p (k t) -> p k t", k=2),
                     xf[b][0][:, 2 * k:2 * k + 2, :]).then_inc(xfl, 1)

        def w13_split(g, f):
            for w in range(2):
                dve.wait_ge(w13h, 2 * GF * g + 2 * f + w + 1)
                split_lo(nc, w13_lo[:, f, w, :, :], w13_raw[:, w, :, f * P:(f + 1) * P],
                         w13_hi[:, f, w, :, :]).then_inc(w13l, 1)

        def w2_split(g):
            dve.wait_ge(w2h, g + 1)
            split_lo(nc, w2_lo[:, :, :], w2_raw[:, :, :], w2_hi[:, :, :]).then_inc(w2l, 1)

        def activate(g, b, f):
            n = 2 * UB * g + UB * b + f
            dve.wait_ge(sil_done, n + 1)
            if not isinstance(g, int) or n >= GF:
                dve.wait_ge(hl, n - 1)
            nc.vector.tensor_tensor(hf[:, f, :], ps[:, 2 * f + 1, :], sil[:, f, :], ALU.mult
                                    ).then_inc(hf_done, 1)
            dve.wait_ge(hh, n + 1)
            split_lo(nc, h_lo[:, b, f, :], hf[:, f, :], h_hi[:, b, f, :]).then_inc(hl, 1)

        def add(g, b):
            for j in range(DB):
                n = 2 * DB * g + DB * b + j
                dve.wait_ge(dn_mm, n + 1)
                if isinstance(g, int) and g % GROUPS == 0:
                    if j == 0:
                        dve.wait_ge(acc_ld[g // GROUPS][b], 16)
                else:
                    dve.wait_ge(acc_done, n + 1 - 2 * DB)
                part_of = acc[:, 4 * b + j // 2, (j % 2) * 512:(j % 2 + 1) * 512]
                nc.vector.tensor_tensor(part_of, ps[:, 4 + j % 4, :], part_of, ALU.add
                                        ).then_inc(acc_done, 1)

        def final_norm(part, b):
            for j in range(4):
                n = part * HT + 4 * b + j
                dve.wait_ge(frs, n + 1)
                nc.vector.scalar_tensor_tensor(out=acc[:, 4 * b + j, :], in0=acc[:, 4 * b + j, :],
                                               scalar=rstd[:, n % 2:n % 2 + 1], in1=gf_b[:, :],
                                               op0=ALU.mult, op1=ALU.mult).then_inc(o_done, 1)

        ys(0, 0)
        for c in ab["chunks"]:
            ab["w_split_lo"](dve, c)
        ys(1, 1)
        ab["conv_rest"](dve, ab["last"])
        dve.wait_ge(g_ld, 16)
        for s in range(2):
            residual(s, s)
            ys(2 + s, s)
            norm(s, s)
        with dve.Fori(1, HT // 2) as i:
            for s in range(2):
                residual(2 * i + s, s, i)
                ys(2 * i + 2 + s, s)
                norm(2 * i + s, s)
        for n in range(HT, TILES - 2):
            residual(n, n % 2, n // 2)
            ys(n + 2, n % 2)
            norm(n, n % 2)
            if HT < n <= HT + XC:
                xf_split(0, 0, n - HT - 1)
        residual(TILES - 2, 0, HT - 1)
        norm(TILES - 2, 0)
        residual(TILES - 1, 1, HT - 1, (0,))
        w13_split(0, 0)
        residual(TILES - 1, 1, HT - 1, (1,))
        norm(TILES - 1, 1)
        w13_split(0, 1)
        for k in range(XC):
            if k == 2:
                activate(0, 0, 0)
            xf_split(0, 1, k)
        w2_split(0)
        activate(0, 0, 1)

        def group(g, more):
            activate(g, 1, 0)
            if more:
                w13_split(g + 1, 0)
            activate(g, 1, 1)
            add(g, 0)
            if more:
                w13_split(g + 1, 1)
                for f in range(GF):
                    activate(g + 1, 0, f)
            add(g, 1)
            if more:
                w2_split(g + 1)

        group(0, True)
        with dve.Fori(1, GROUPS - 1) as i:
            group(i, True)
        g = GROUPS - 1
        for k in range(XC):
            xf_split(1, 0, k)
        activate(g, 1, 0)
        w13_split(g + 1, 0)
        activate(g, 1, 1)
        add(g, 0)
        w13_split(g + 1, 1)
        for k in range(XC):
            xf_split(1, 1, k)
        dve.wait_ge(gf_ld, 16)
        final_norm(0, 0)
        for f in range(GF):
            activate(g + 1, 0, f)
        add(g, 1)
        w2_split(g + 1)
        final_norm(0, 1)
        group(GROUPS, True)
        with dve.Fori(GROUPS + 1, LAST - 1) as i:
            group(i, True)
        g = LAST - 1
        activate(g, 1, 0)
        activate(g, 1, 1)
        add(g, 0)
        final_norm(1, 0)
        add(g, 1)
        final_norm(1, 1)

    @block.tensor
    def _(pe):
        def products(n, s, halves=range(2)):
            for b in halves:
                if isinstance(n, int) and n == 0:
                    pe.wait_ge(ab["wlo"], ab["n_wlo"][b])
                if later(n):
                    pe.wait_ge(xm_done, 2 * (n - 2) + b + 1)
                for k in range(KT):
                    if b == 0 and k == 0:
                        pe.wait_ge(ys_l, n + 1)
                    if b == 0 and k == 2 * CT:
                        pe.wait_ge(yf_l, n + 1)
                    a, w = (ys_hi[:, s, k, :], ys_lo[:, s, k, :]), (wo[b][0][:, k, :], wo[b][1][:, k, :])
                    out = ps[:, 2 * s + b, :]
                    nc.tensor.matmul(out, a[0], w[0], start=(k == 0), stop=False)
                    nc.tensor.matmul(out, a[0], w[1], start=False, stop=False)
                    ins = nc.tensor.matmul(out, a[1], w[0], start=False, stop=(k == KT - 1))
                ins.then_inc(o_mm, 1)

        def transposes(n, s):
            pe.wait_ge(xn_done, n + 1)
            if later(n):
                pe.wait_ge(xt_done, n - 1)
            for k in range(KT):
                ins = nc.tensor.transpose(ps[:, 4 + 2 * s + k // 4, (k % 4) * P:(k % 4 + 1) * P],
                                          xn[:, s, k * P:(k + 1) * P], ident[:, :])
            ins.then_inc(tr_done, 1)

        for b in range(2):
            products(0, 0, (b,))
            products(1, 1, (b,))
        pe.wait_ge(ab["act_ev"], ab["n_act_ev"])
        pe.wait_ge(ab["dve_ev"], ab["n_dve_ev"])
        transposes(0, 0)
        products(2, 0)
        transposes(1, 1)
        with pe.Fori(1, TILES // 2 - 1) as i:
            products(2 * i + 1, 1)
            transposes(2 * i, 0)
            products(2 * i + 2, 0)
            transposes(2 * i + 1, 1)
        products(TILES - 1, 1)
        transposes(TILES - 2, 0)

        def up(g, b):
            for f in range(GF):
                n = 2 * UB * g + UB * b + f
                for w in range(2):
                    if b == 0:
                        pe.wait_ge(w13l, 2 * GF * g + 2 * f + w + 1)
                    if not isinstance(g, int) or n >= GF:
                        pe.wait_ge((sil_done, hf_done)[w], n - 1)
                    elif n == 0 and w == 0:
                        pe.wait_ge(xm_done, 2 * TILES)
                    if isinstance(g, int) and g % GROUPS == 0 and f == 0 and w == 0:
                        pe.wait_ge(xfl, (2 * (g // GROUPS) + b + 1) * XC)
                    ins = mm3(nc, ps[:, 2 * f + w, :],
                              [((w13_hi[:, f, w, k, :], w13_lo[:, f, w, k, :]),
                                (xf[b][0][:, k, :], xf[b][1][:, k, :])) for k in range(KT)])
                    if isinstance(g, int) and n == 0 and w == 0:
                        transposes(TILES - 1, 1)
                ins.then_inc(up_mm, 1)

        def down(g, b):
            pe.wait_ge(hl, 2 * UB * g + UB * b + UB)
            if b == 0:
                pe.wait_ge(w2l, g + 1)
            for j in range(DB):
                n = 2 * DB * g + DB * b + j
                if not isinstance(g, int) or n >= 4:
                    pe.wait_ge(acc_done, n - 3)
                elif n == 0:
                    pe.wait_ge(xt_done, TILES)
                tok = slice((j // 2) * P, (j // 2 + 1) * P)
                col = slice((j % 2) * 512, (j % 2 + 1) * 512)
                mm3(nc, ps[:, 4 + j % 4, :],
                    [((h_hi[:, b, f, tok], h_lo[:, b, f, tok]), (w2_hi[:, f, col], w2_lo[:, f, col]))
                     for f in range(GF)]).then_inc(dn_mm, 1)

        def group(g):
            up(g, 1)
            down(g, 0)
            up(g + 1, 0)
            down(g, 1)

        up(0, 0)
        group(0)
        with pe.Fori(1, GROUPS - 1) as i:
            group(i)
        group(GROUPS - 1)
        group(GROUPS)
        with pe.Fori(GROUPS + 1, LAST - 1) as i:
            group(i)
        up(LAST - 1, 1)
        down(LAST - 1, 0)
        down(LAST - 1, 1)


def encoder_layer(nc, t):
    with Alloc(nc) as m:
        (ident,) = place(nc, AT_SMALL, ("ident", [P, P]))
        (uf,) = place(nc, AT_UF, ("uf", [P, FT, S]))
        ps = m.stack.enter_context(nc.psum_tensor("ps", [P, 8, 512], F32))
        block = m.block()
        ab = stage_ab(nc, t, m, block, ident, ps, uf)
        stage_cd(nc, t, m, block, ident, ps, uf, ab)


def shape_constants():
    import numpy as np
    hd = 64
    j = np.arange(hd)
    ang = 2 * np.pi * np.outer(j, j) / hd
    norm = 1.0 / np.sqrt(S * hd)
    dft64 = np.zeros((P, 2, P))
    for f, mat in enumerate((np.cos(ang), np.sin(ang))):
        for h in range(2):
            dft64[hd * h:hd * h + hd, f, hd * h:hd * h + hd] = mat * norm
    n2 = np.arange(P)[:, None, None]
    n1 = np.arange(R1)[None, :, None]
    k2 = np.arange(P)[None, None, :]
    ang = 2 * np.pi * (((n1 + R1 * n2) * k2) % S) / S
    tw = np.stack([np.cos(ang), np.sin(ang)], axis=2)
    t16 = np.zeros((4, R1, 2, R1, 4))
    k1 = np.arange(R1)
    ang = 2 * np.pi * (np.outer(k1, k1) % R1) / R1
    for a in range(4):
        t16[a, :, 0, :, a] = np.cos(ang)
        t16[a, :, 1, :, a] = -np.sin(ang)
    windows = np.repeat([2, 4, 8, 16], 96)
    tok = np.concatenate([np.arange(PAD), np.arange(S - PAD, S)])
    cnt = (np.minimum(tok + windows[:, None] // 2, S) - np.maximum(tok - windows[:, None] // 2, 0))
    f = np.float32
    return {
        "ident": np.eye(P, dtype=f), "dft64": dft64.astype(f), "tw": tw.astype(f),
        "t16": t16.reshape(P, 64).astype(f),
        "invw": np.ascontiguousarray((1.0 / windows).reshape(CT, P).T).astype(f),
        "invcnt": np.ascontiguousarray((1.0 / cnt).reshape(CT, P, 2 * PAD).transpose(1, 0, 2)).astype(f),
    }


_INS = ["x", "g_mix", "w_in", "w_fourier", "w_pool", "w_out", "g_ffn", "w1", "w3", "w2"]


def kernel(**inputs):
    import numpy as np
    import concourse.bacc as bacc
    from concourse.bass_utils import run_bass_kernel_spmd

    nc = bacc.Bacc("TRN2", target_bir_lowering=False, num_devices=1)
    arrays = {n: np.ascontiguousarray(inputs[n]) for n in _INS}
    arrays["g_final"] = np.ascontiguousarray(inputs["g_final"]).reshape(1, D)
    arrays["wconv"] = np.ascontiguousarray(np.asarray(inputs["w_conv"]).reshape(3, CT, P).transpose(2, 1, 0))
    arrays["pscale"] = np.ascontiguousarray(np.asarray(inputs["pool_scale"]).reshape(CT, P).T)
    arrays.update(shape_constants())
    t = {n: nc.dram_tensor(f"in_{n}", a.shape, mybir.dt.from_np(a.dtype), kind="ExternalInput").ap()
         for n, a in arrays.items()}
    t["out"] = nc.dram_tensor("out", (1, S, D), F32, kind="ExternalOutput").ap()
    for n, shape in (("yd", (P, 2 * CT, S)), ("g", (P, R1, 4 * P)),
                     ("xmid", (TILES, P, D)), ("xt", (P, KT, S))):
        t[n] = nc.dram_tensor(f"scratch_{n}", shape, F32, kind="Internal").ap()
    encoder_layer(nc, t)
    r = run_bass_kernel_spmd(nc, [{f"in_{n}": a for n, a in arrays.items()}], core_ids=[0])
    return r.results[0]["out"]
```
